# Optimizing a Trainium2 kernel written in Bass

```python
import jax, jax.numpy as jnp
from jax import lax
import numpy as np

D_MODEL = 1024
BATCH = 1
SEQ = 512
DEPTH = 1

CHUNK = 64
D_MIX = D_MODEL
HEAD_DIM = 64
RWKV_DIM = D_MIX // 4
RWKV_HEADS = RWKV_DIM // HEAD_DIM
RWKV_W_LORA = 64
RWKV_A_LORA = 64
RWKV_G_LORA = 128
RWKV_GN_EPS = 64e-5
POOL_DIM = D_MIX // 4
POOL_WINDOWS = (2, 4, 8, 16)
POOL_GROUP = POOL_DIM // len(POOL_WINDOWS)
FOX_DIM = D_MIX - RWKV_DIM - POOL_DIM
FOX_HEADS = FOX_DIM // HEAD_DIM
QUERY_BLOCK = 128
N_EXPERTS = 32
TOP_K = 4
D_FF = D_MODEL
SWIGLU_LIMIT = 7.0
SWIGLU_ALPHA = 1.702
EXPERT_BLOCK = 128
NORM_EPS = 1e-6
RWKV_IN = 3 * RWKV_DIM + RWKV_W_LORA + RWKV_A_LORA + RWKV_G_LORA
FOX_IN = 3 * FOX_DIM + FOX_HEADS
P_IN = RWKV_IN + POOL_DIM + FOX_IN

kernel_name = "hybrid_rwkv7_pool_fox_moe_adaln"

def _f32(t):
    return t.astype(jnp.float32)

def rms_norm(x, g):
    xf = _f32(x)
    y = xf * lax.rsqrt(jnp.mean(xf * xf, axis=-1, keepdims=True) + NORM_EPS)
    return (y * _f32(g)).astype(x.dtype)

def rwkv7_mixer(z, mu, w0, w_up, a0, a_up, g_up, k_k, k_a, r_k, ln_w, ln_b):
    B, S, _ = z.shape
    H, N = RWKV_HEADS, HEAD_DIM
    zf = _f32(z)
    prev = jnp.pad(zf, ((0, 0), (1, 0), (0, 0)))[:, :S]
    zf = zf + (prev - zf) * _f32(mu)
    cuts = [RWKV_DIM, 2 * RWKV_DIM, 3 * RWKV_DIM, 3 * RWKV_DIM + RWKV_W_LORA,
            3 * RWKV_DIM + RWKV_W_LORA + RWKV_A_LORA]
    r, k, v, wd, ad, gd = jnp.split(zf, cuts, axis=-1)
    w_log = -jax.nn.softplus(-(_f32(w0) + jnp.tanh(wd) @ _f32(w_up))) - 0.5
    decay = jnp.exp(-jnp.exp(w_log))
    a = jax.nn.sigmoid(_f32(a0) + ad @ _f32(a_up))
    g = jax.nn.sigmoid(gd) @ _f32(g_up)
    heads = lambda t: t.reshape(B, S, H, N)
    kk = heads(k * _f32(k_k))
    kk = kk / jnp.maximum(jnp.sqrt(jnp.sum(kk * kk, axis=-1, keepdims=True)), 1e-12)
    k = k * (1.0 + (a - 1.0) * _f32(k_a))
    r_h, k_h, v_h, w_h, a_h = heads(r), heads(k), heads(v), heads(decay), heads(a)

    def step(state, inp):
        r_t, w_t, k_t, v_t, kk_t, a_t = inp
        sa = jnp.einsum('bhvk,bhk->bhv', state, -kk_t)
        state = (state * w_t[:, :, None, :]
                 + sa[..., None] * (kk_t * a_t)[:, :, None, :]
                 + v_t[..., None] * k_t[:, :, None, :])
        return state, jnp.einsum('bhvk,bhk->bhv', state, r_t)

    xs = tuple(jnp.moveaxis(t, 1, 0) for t in (r_h, w_h, k_h, v_h, kk, a_h))
    s0 = jnp.zeros((B, H, N, N), jnp.float32)
    _, y = lax.scan(step, s0, xs)
    y = jnp.moveaxis(y, 0, 1)
    mean = jnp.mean(y, axis=-1, keepdims=True)
    var = jnp.mean(jnp.square(y - mean), axis=-1, keepdims=True)
    y = (y - mean) * lax.rsqrt(var + RWKV_GN_EPS) * _f32(ln_w).reshape(H, N) + _f32(ln_b).reshape(H, N)
    y = y + jnp.sum(r_h * k_h * _f32(r_k), axis=-1, keepdims=True) * v_h
    return (y.reshape(B, S, RWKV_DIM) * g).astype(z.dtype)

def pool_mixer(z, w_pool, scale):
    B, S, _ = z.shape
    zg = _f32(z).reshape(B, S, len(POOL_WINDOWS), POOL_GROUP)
    cs = jnp.cumsum(zg, axis=1)
    count = jnp.arange(1, S + 1, dtype=jnp.float32)
    outs = []
    for gi, w in enumerate(POOL_WINDOWS):
        c_g = cs[:, :, gi]
        lagged = jnp.pad(c_g, ((0, 0), (w, 0), (0, 0)))[:, :S]
        mean = (c_g - lagged) / jnp.minimum(count, w)[None, :, None]
        outs.append(mean - zg[:, :, gi])
    pooled = jnp.stack(outs, axis=2)
    y = jnp.einsum('bsgc,gcd->bsgd', pooled, _f32(w_pool)).reshape(B, S, POOL_DIM) * _f32(scale)
    return y.astype(z.dtype)

def fox_mixer(z, b_f):
    B, S, _ = z.shape
    H, Dh = FOX_HEADS, HEAD_DIM
    to_heads = lambda t: t.reshape(B, S, H, Dh).transpose(0, 2, 1, 3)
    q = to_heads(z[..., :FOX_DIM])
    k = to_heads(z[..., FOX_DIM:2 * FOX_DIM])
    v = to_heads(z[..., 2 * FOX_DIM:3 * FOX_DIM])
    log_f = jax.nn.log_sigmoid(_f32(z[..., 3 * FOX_DIM:]) + _f32(b_f))
    cum = jnp.cumsum(log_f, axis=1).transpose(0, 2, 1)
    nq = S // QUERY_BLOCK
    q_blocks = q.reshape(B, H, nq, QUERY_BLOCK, Dh).transpose(2, 0, 1, 3, 4)
    c_blocks = cum.reshape(B, H, nq, QUERY_BLOCK).transpose(2, 0, 1, 3)
    key_pos = jnp.arange(S)
    sm_scale = HEAD_DIM ** -0.5

    def block(args):
        q_blk, c_blk, i = args
        s = (_f32(jnp.einsum('bhqd,bhkd->bhqk', q_blk, k)) * sm_scale
             + (c_blk[..., None] - cum[:, :, None, :]))
        q_pos = i * QUERY_BLOCK + jnp.arange(QUERY_BLOCK)
        s = jnp.where(key_pos[None, :] <= q_pos[:, None], s, -jnp.inf)
        p = jax.nn.softmax(s, axis=-1)
        return jnp.einsum('bhqk,bhkd->bhqd', p.astype(v.dtype), v)

    o = lax.map(block, (q_blocks, c_blocks, jnp.arange(nq)))
    return o.transpose(1, 0, 3, 2, 4).reshape(B, S, FOX_DIM).astype(z.dtype)

def moe_ffn(h, router_w, router_b, w_gu, b_gu, w_down, b_down):
    B, S, D = h.shape
    N = B * S
    NK = N * TOP_K
    xf = h.reshape(N, D)
    logits = _f32(xf @ router_w + router_b)
    top_v, top_i = lax.top_k(logits, TOP_K)
    gates = jax.nn.softmax(top_v, axis=-1)
    e_flat = top_i.reshape(NK).astype(jnp.int32)
    g_flat = gates.reshape(NK)
    order = jnp.argsort(e_flat)
    se = e_flat[order]
    stok = (order // TOP_K).astype(jnp.int32)
    sg = g_flat[order]
    counts = jnp.bincount(e_flat, length=N_EXPERTS).astype(jnp.int32)
    padded = (counts + EXPERT_BLOCK - 1) // EXPERT_BLOCK * EXPERT_BLOCK
    pend = jnp.cumsum(padded)
    pstart = pend - padded
    gstart = jnp.cumsum(counts) - counts
    dest = pstart[se] + jnp.arange(NK, dtype=jnp.int32) - gstart[se]
    nb = -(-(NK + N_EXPERTS * (EXPERT_BLOCK - 1)) // EXPERT_BLOCK)
    rows = nb * EXPERT_BLOCK
    row_tok = jnp.zeros((rows,), jnp.int32).at[dest].set(stok)
    block_e = jnp.minimum(
        jnp.searchsorted(pend, jnp.arange(nb, dtype=jnp.int32) * EXPERT_BLOCK, side='right'),
        N_EXPERTS - 1).astype(jnp.int32)
    xb = xf[row_tok].reshape(nb, EXPERT_BLOCK, D)

    def expert_block(args):
        x_blk, e = args
        gu = x_blk @ w_gu[e] + b_gu[e]
        gate = jnp.minimum(gu[:, :D_FF], SWIGLU_LIMIT)
        up = jnp.clip(gu[:, D_FF:], -SWIGLU_LIMIT, SWIGLU_LIMIT)
        act = (up + 1.0) * (gate * jax.nn.sigmoid(SWIGLU_ALPHA * gate))
        return act @ w_down[e] + b_down[e]

    yb = lax.map(expert_block, (xb, block_e)).reshape(rows, D)
    y = jnp.zeros((N, D), h.dtype).at[stok].add(yb[dest] * sg[:, None].astype(h.dtype))
    return y.reshape(B, S, D)

def setup_inputs(seed: int = 0) -> dict:
    key = jax.random.key(seed)
    ks = iter(jax.random.split(key, 40))
    nrm = lambda shape, s: jax.random.normal(next(ks), shape, jnp.float32) * s
    L, D, E = DEPTH, D_MODEL, N_EXPERTS
    return {
        "x": nrm((BATCH, SEQ, D), 1.0),
        "c": nrm((BATCH, D), 1.0),
        "ada_w": nrm((L, D, 6 * D), 0.5 * D ** -0.5),
        "ada_b": nrm((L, 6 * D), 0.02),
        "norm1": 1.0 + nrm((L, D), 0.05),
        "w_in": nrm((L, D, P_IN), D ** -0.5),
        "w_out": nrm((L, D_MIX, D), D_MIX ** -0.5),
        "rwkv_mu": 0.5 + nrm((L, RWKV_IN), 0.1),
        "rwkv_w0": -2.5 + nrm((L, RWKV_DIM), 1.0),
        "rwkv_w_up": nrm((L, RWKV_W_LORA, RWKV_DIM), 0.5 * RWKV_W_LORA ** -0.5),
        "rwkv_a0": nrm((L, RWKV_DIM), 0.1),
        "rwkv_a_up": nrm((L, RWKV_A_LORA, RWKV_DIM), 0.5 * RWKV_A_LORA ** -0.5),
        "rwkv_g_up": nrm((L, RWKV_G_LORA, RWKV_DIM), RWKV_G_LORA ** -0.5),
        "rwkv_k_k": 0.85 + nrm((L, RWKV_DIM), 0.05),
        "rwkv_k_a": 1.0 + nrm((L, RWKV_DIM), 0.05),
        "rwkv_r_k": nrm((L, RWKV_HEADS, HEAD_DIM), 0.1),
        "rwkv_ln_w": 1.0 + nrm((L, RWKV_DIM), 0.05),
        "rwkv_ln_b": nrm((L, RWKV_DIM), 0.02),
        "pool_w": nrm((L, len(POOL_WINDOWS), POOL_GROUP, POOL_GROUP), POOL_GROUP ** -0.5),
        "pool_scale": 1.0 + nrm((L, POOL_DIM), 0.1),
        "fox_b_f": 2.0 + nrm((L, FOX_HEADS), 1.0),
        "norm2": 1.0 + nrm((L, D), 0.05),
        "router_w": nrm((L, D, E), D ** -0.5),
        "router_b": nrm((L, E), 0.01),
        "moe_w_gu": nrm((L, E, D, 2 * D_FF), D ** -0.5),
        "moe_b_gu": nrm((L, E, 2 * D_FF), 0.01),
        "moe_w_down": nrm((L, E, D_FF, D), D_FF ** -0.5),
        "moe_b_down": nrm((L, E, D), 0.01),
        "norm_f": 1.0 + nrm((D,), 0.05),
    }

def reference(x, c, ada_w, ada_b, norm1, w_in, w_out, rwkv_mu, rwkv_w0, rwkv_w_up, rwkv_a0,
              rwkv_a_up, rwkv_g_up, rwkv_k_k, rwkv_k_a, rwkv_r_k, rwkv_ln_w, rwkv_ln_b,
              pool_w, pool_scale, fox_b_f, norm2, router_w, router_b, moe_w_gu, moe_b_gu,
              moe_w_down, moe_b_down, norm_f):
    cond = jax.nn.silu(c)
    for l in range(DEPTH):
        mod = (cond @ ada_w[l] + ada_b[l])[:, None, :]
        sh1, sc1, g1, sh2, sc2, g2 = jnp.split(mod, 6, axis=-1)
        h = rms_norm(x, norm1[l]) * (1.0 + sc1) + sh1
        zp = h @ w_in[l]
        z_rwkv = zp[..., :RWKV_IN]
        z_pool = zp[..., RWKV_IN:RWKV_IN + POOL_DIM]
        z_fox = zp[..., RWKV_IN + POOL_DIM:]
        y_rwkv = rwkv7_mixer(z_rwkv, rwkv_mu[l], rwkv_w0[l], rwkv_w_up[l], rwkv_a0[l], rwkv_a_up[l],
                             rwkv_g_up[l], rwkv_k_k[l], rwkv_k_a[l], rwkv_r_k[l], rwkv_ln_w[l],
                             rwkv_ln_b[l])
        y_pool = pool_mixer(z_pool, pool_w[l], pool_scale[l])
        y_fox = fox_mixer(z_fox, fox_b_f[l])
        mixed = jnp.concatenate([y_rwkv, y_pool, y_fox], axis=-1)
        x = x + g1 * (mixed @ w_out[l])
        h = rms_norm(x, norm2[l]) * (1.0 + sc2) + sh2
        x = x + g2 * moe_ffn(h, router_w[l], router_b[l], moe_w_gu[l], moe_b_gu[l],
                             moe_w_down[l], moe_b_down[l])
    return rms_norm(x, norm_f)


_drawn_inputs = setup_inputs


def setup_inputs(seed=0):
    import zlib

    import numpy as np

    out = dict(_drawn_inputs(seed))
    spreads = {}
    factors = {'norm1': 3.493,
     'rwkv_w_up': 5.399,
     'rwkv_a0': 6.611,
     'rwkv_a_up': 2.755,
     'rwkv_k_k': 50.792,
     'rwkv_k_a': 5.164,
     'rwkv_ln_w': 38.089,
     'rwkv_ln_b': 64.0,
     'pool_scale': 2.946,
     'router_b': 46.776,
     'moe_b_gu': 64.0,
     'moe_b_down': 64.0,
     'norm2': 7.539}
    for name, (base, spread) in spreads.items():
        noise = np.random.default_rng([zlib.crc32(name.encode()), seed]).standard_normal(out[name].shape)
        drawn = base * np.exp(spread * noise) if base else spread * noise
        out[name] = __import__('jax').numpy.asarray(drawn.astype(out[name].dtype))
    for name, factor in factors.items():
        out[name] = (out[name] * factor).astype(out[name].dtype)
    return out
```

```python
from contextlib import ExitStack

import numpy as np
import concourse.bass as bass
from concourse import mybir

F32 = mybir.dt.float32
BF16 = mybir.dt.bfloat16
I32 = mybir.dt.int32
U32 = mybir.dt.uint32
ALU = mybir.AluOpType
ACT = mybir.ActivationFunctionType
AX_X = mybir.AxisListType.X

P = 128
D = 1024
S = 512
KT = D // P
TT = S // P
HD = 64
RW = 256
RH = RW // HD
CT = RW // P
CHUNK = 64
NC = S // CHUNK
POOL_WINDOWS = (2, 4, 8, 16)
PAD = max(POOL_WINDOWS)
FOX = 512
FH = FOX // HD
RWKV_IN = 1024
COL_POOL = RWKV_IN
COL_Q = COL_POOL + 256
COL_K = COL_Q + FOX
COL_V = COL_K + FOX
COL_F = COL_V + FOX
E = 32
TOPK = 4
F = 1024
BLK = 128
MAXOV = 15
NB = E + MAXOV
NORM_EPS = 1e-6
GN_EPS = 64e-5
DECAY = -float(np.exp(-0.5))
SM = HD ** -0.5
LEVELS = 6

READERS = {"ada": "D", "hT": "A", "rw": "A", "q": "A", "lora": "A", "k": "A", "kkn": "A", "rk": "D",
           "v": "A", "pz": "A", "f": "AD", "pm": "A", "trAV": "A", "trBK": "D",
           "MP": "AD", "NP": "D", "M": "D", "T": "A", "XA": "D", "XB": "D", "NV": "A", "W": "A",
           "QY": "AD", "GH": "A"}
JOB_BANKS = 3


def plan():
    steps = [("ada", b) for b in range(4)]
    steps += [("hT", t, half) for t in range(TT) for half in range(2)]
    steps += [("rw", n) for n in range(8)]
    steps += [("q", n) for n in range(4)]
    steps += [("lora", n) for n in range(6)]
    steps += [("k", n) for n in range(4)]
    steps += [("kkn", ct) for ct in range(CT)] + [("rk", ct) for ct in range(CT)]
    steps += [("v", t) for t in range(TT)]
    steps += [("pz", 0), ("pz", 1), ("f", 0)]
    steps += [("ada", b) for b in range(4, 8)] + [("pm", 0)] + [("ada", b) for b in range(8, 12)]
    steps += [("trAV", t) for t in range(TT)] + [("trBK", t) for t in range(TT)] + [("pm", 1)]
    solve = []
    for q in range(2):
        for j in range(2):
            t = 2 * q + j
            solve += [(kind, t, par) for kind in ("MP", "M", "NP") for par in range(2)]
        for lv in range(1, LEVELS):
            solve += [("T", 2 * q + j, lv) for j in range(2)]
            for j in range(2):
                if lv < LEVELS - 1:
                    solve.append(("XA", 2 * q + j, lv))
                solve.append(("XB", 2 * q + j, lv))
        for kind in ("NV", "W", "QY"):
            solve += [(kind, 2 * q + j) for j in range(2)]
        solve += [("GH", 2 * q + j, cc) for j in range(2) for cc in range(2)]
    units = FH * TT
    done = 0
    for n, s in enumerate(solve):
        steps.append(s)
        while done * len(solve) < (n + 1) * (units + 2):
            steps.append(("fox", done))
            done += 1
    while done < units + 2:
        steps.append(("fox", done))
        done += 1
    return steps


STEPS = plan()
JOBS = [s for s in STEPS if s[0] != "fox"]
JOB = {s: n for n, s in enumerate(JOBS)}


def reads_through(engine, job):
    return sum(engine in READERS[s[0]] for s in JOBS[:JOB[job] + 1])


def build(nc, a, out):
    with ExitStack() as ctx:
        def sb(name, shape, dt=F32):
            return ctx.enter_context(nc.sbuf_tensor(name, shape, dt))

        def sem(name):
            return ctx.enter_context(nc.semaphore(name))

        Wt = sb("Wt", [P, 24576])
        R = sb("R", [P, 25248])
        W3 = lambda off, x, y: Wt[:, off:off + x * y].rearrange("p (x y) -> p x y", x=x)
        R3 = lambda off, x, y: R[:, off:off + x * y].rearrange("p (x y) -> p x y", x=x)

        blk = [W3(4096 * s, KT, 512) for s in range(2)]
        def pair(off):
            return [W3(off + 512 * j, RH, P) for j in range(2)]
        MT, X, XT, Tm, ML, NT, PbT, PkT = [pair(1024 * n) for n in range(8)]
        W12 = [m.rearrange("p h (w k) -> p h w k", w=2) for m in ML]
        QT = W3(8192, CT, S)
        Yin = W3(9216, CT, S)
        GH = Wt[:, 10240:12288].rearrange("p (x c m) -> p x c m", x=CT, c=NC)
        tokA, tokV, tokB, tokK = [W3(12288 + 1024 * n, TT, RW) for n in range(4)]
        AR = Wt[:, 16384:18432].rearrange("p (x w t) -> p x w t", x=CT, w=2)
        Bt = W3(18432, CT, S)
        Kt = W3(19456, CT, S)
        Kh = W3(20480, CT, S)
        Bh = W3(21504, CT, S)
        L = W3(22528, CT, S)
        WG = W3(23552, 2, S)
        w_out_sb = W3(16384, KT, D)
        htmp = W3(16384, 2, D)
        norm1B = Wt[:, 18432:19456]
        lnY, lnC, lnS = [W3(1024 * n, CT, S) for n in range(3)]

        mod = R3(0, 6, D)
        gT = R3(0, CT, S)
        rkv = R3(1024, CT, S)
        condB = R3(6144, KT, P)
        x_sb = R3(7168, TT, D)
        rT, kT, vT, aT = [R3(7168 + 1024 * n, CT, S) for n in range(4)]
        hT = R3(11264, KT, S)
        Pm = R3(11264, 2, S)
        PT = R3(12288, 2, S)
        tA = R[:, 13312:13840]
        tB = R[:, 13840:14368]
        fq = R3(15360, 4, S)
        fk = R3(17408, 4, S)
        fv = R3(19456, TT, FOX)
        cum = R[:, 21504:22016]
        fln = R[:, 22016:22528]
        pz = R3(22528, CT, S + PAD)
        pmix = R3(22528, CT, S)
        ST = R[:, 23584:24736].rearrange("p (x c v) -> p x c v", x=CT, c=9)
        fmin = R[:, 24736:25248]
        zraw = R[:, 23584:24612].rearrange("p (b t) -> p b t", b=2)

        ident = sb("ident", [P, P])
        identb = sb("identb", [P, P], BF16)
        blockones = sb("blockones", [P, P])
        causal = sb("causal", [P, P], BF16)
        lvl = sb("lvl", [P, LEVELS, P])
        strict = sb("strict", [P, P])
        incl = sb("incl", [P, P])
        lvl0T = sb("lvl0T", [P, P])
        negsel = sb("negsel", [8, 8])
        scanmask = sb("scanmask", [P, S], BF16)
        cols = sb("cols", [P, 25])
        MU, W0, A0, KK_, KA, RK, LNW, LNB, PSC = 0, 8, 10, 12, 14, 16, 18, 20, 22
        up = sb("up", [P, RW])
        g_up = sb("g_up", [P, RW])
        pool_w = sb("pool_w", [P, CT, HD])
        cT = sb("cT", [P, KT])
        cs = sb("cs", [P, KT])
        rcnt = sb("rcnt", [P, CT, PAD])
        fix = sb("fix", [P, PAD])
        ss = sb("ss", [P, TT])
        rstd = sb("rstd", [P, TT])
        gam = sb("gam", [P, CT, NC])
        fmx = sb("fmx", [P, 8])
        stmp = sb("stmp", [P, CT, HD])
        strictb = sb("strictb", [P, P], BF16)
        onesb = sb("onesb", [P, P], BF16)
        bsel = sb("bsel", [3 * E, E], BF16)
        iotaE = sb("iotaE", [P, E])
        iotaJ = sb("iotaJ", [P, MAXOV])
        zeroE = sb("zeroE", [P, E])
        zero_tab = sb("zero_tab", [P, NB], U32)
        tokid = sb("tokid", [P, TT], U32)
        rw_sb = R3(6144, KT, E)
        rb = R[:, 6400:6432]
        lgs = R3(6432, TT, E)
        top = R3(6560, TT, 8)
        idxu = R3(6592, TT, 8).bitcast(U32)
        idxf = R3(6624, TT, 8)
        maskb = R[:, 6656:6720].bitcast(BF16).rearrange("p (t e) -> p t e", t=TT)
        rank = R[:, 6720:6848]
        rge = R[:, 6848:6976]
        cnt = R[:, 6976:7008]
        ovf = R[:, 7008:7040]
        ovc = R[:, 7040:7072]
        slotf = R[:, 7072:7088]
        tf = R[:, 7088:7104]
        ovx = R[:, 7104:7120]
        gsum = R[:, 7120:7124]
        oh = R[:, 24736:25248].rearrange("p (t k e) -> p t k e", t=TT, k=TOPK)
        slotI = sb("slotI", [P, TT * TOPK], U32)
        ti = sb("ti", [P, TT * TOPK], U32)
        tabI = sb("tabI", [P, TT * TOPK], U32)
        ovI = sb("ovI", [P, MAXOV + 1], I32)
        tok = sb("tok", [P, NB], U32)
        icol = [sb(f"icol{s}", [P, 1], U32) for s in range(2)]
        gates = sb("gates", [P, TT, TOPK])
        carried = sb("carried", [P, 2])
        braw = R[0:E, 17408:20480]
        norm2B = R[:, 14336:15360]
        xi = Wt[:, 0:P].bitcast(I32)
        yi = Wt[:, P:2 * P].bitcast(I32)

        h2_d = nc.dram_tensor("h2_rows", (S, D), F32, kind="Internal").ap()
        y_d = nc.dram_tensor("y_rows", (NB * BLK, D), F32, kind="Internal").ap()
        tab_d = nc.dram_tensor("slot_token", (P * NB, 1), U32, kind="Internal").ap()

        ps = ctx.enter_context(nc.psum_tensor("ps", [P, 8, 512], F32))
        job_bank = lambda job: ps[:, JOB[job] % JOB_BANKS, :]
        fox_s = lambda u: ps[:, 3 + u % 2, :]
        fox_t = lambda u: ps[:, 5 + u % 2, :]
        fox_o = ps[:, 7, :]

        x_in = sem("x_in")
        small_in = sem("small_in")
        bias_in = sem("bias_in")
        blk_in = [sem(f"blk_in{s}") for s in range(2)]
        wout_in = sem("wout_in")
        cst_pool = sem("cst_pool")
        cst_dve = sem("cst_dve")
        cond_sig = sem("cond_sig")
        cond_rdy = sem("cond_rdy")
        sq_done = sem("sq_done")
        h_add = sem("h_add")
        ms_rdy = sem("ms_rdy")
        rms_rdy = sem("rms_rdy")
        var_rdy = sem("var_rdy")
        std_rdy = sem("std_rdy")
        job_mm = sem("job_mm")
        act_read = sem("act_read")
        dve_read = sem("dve_read")
        dve_chain = sem("dve_chain")
        act_chain = sem("act_chain")
        pool_chain = sem("pool_chain")
        shifted = sem("shifted")
        lora_in = sem("lora_in")
        kk_raw = sem("kk_raw")
        kk_sq = sem("kk_sq")
        rk_in = sem("rk_in")
        logs = sem("logs")
        exps = sem("exps")
        elem_dve = sem("elem_dve")
        kk_unit = sem("kk_unit")
        elem_pool = sem("elem_pool")
        pool_sum = sem("pool_sum")
        pooled = sem("pooled")
        f_ln = sem("f_ln")
        cum_rdy = sem("cum_rdy")
        solve_pool = sem("solve_pool")
        fox_sc = sem("fox_sc")
        fox_mx = sem("fox_mx")
        fox_ex = sem("fox_ex")
        fox_nm = sem("fox_nm")
        fox_tr = sem("fox_tr")
        fox_pa = sem("fox_pa")
        fox_pd = sem("fox_pd")
        fox_pv = sem("fox_pv")
        fox_oe = sem("fox_oe")
        st_zero = sem("st_zero")
        st_mm = sem("st_mm")
        st_new = sem("st_new")
        y_mm = sem("y_mm")
        y_sum = sem("y_sum")
        mean_mm = sem("mean_mm")
        y_cen = sem("y_cen")
        y_sq = sem("y_sq")
        var_mm = sem("var_mm")
        y_scl = sem("y_scl")
        y_aff = sem("y_aff")
        rw_out = sem("rw_out")
        small2_in = sem("small2_in")
        normf_in = sem("normf_in")
        p_mm = sem("p_mm")
        x2_rdy = sem("x2_rdy")
        sq2_done = sem("sq2_done")
        ms2_rdy = sem("ms2_rdy")
        rms2_rdy = sem("rms2_rdy")
        h2_rdy = sem("h2_rdy")
        h2t_mm = sem("h2t_mm")
        h2t_ev = sem("h2t_ev")
        lg_mm = sem("lg_mm")
        gdif_rdy = sem("gdif_rdy")
        gexp_rdy = sem("gexp_rdy")
        mask_rdy = sem("mask_rdy")
        rank_mm = sem("rank_mm")
        slots_rdy = sem("slots_rdy")
        ov_rdy = sem("ov_rdy")
        tab_zero = sem("tab_zero")
        y_zero = sem("y_zero")
        scat = sem("scat")
        tok_in = sem("tok_in")
        ic_rdy = sem("ic_rdy")
        xt_mm = sem("xt_mm")
        xt_ev = sem("xt_ev")
        gu_used = sem("gu_used")
        dn_used = sem("dn_used")
        sw_rd = sem("sw_rd")
        g_rdy = sem("g_rdy")
        sig_rdy = sem("sig_rdy")
        gs_rdy = sem("gs_rdy")
        act_rdy = sem("act_rdy")
        at_mm = sem("at_mm")
        at_ev = sem("at_ev")
        y_ev = sem("y_ev")
        x3_rdy = sem("x3_rdy")
        sq3_done = sem("sq3_done")
        ms3_rdy = sem("ms3_rdy")
        rms3_rdy = sem("rms3_rdy")
        res_rdy = sem("res_rdy")
        comb_done = sem("comb_done")
        dve_chain2 = sem("dve_chain2")
        h2_out = [sem(f"h2_out{s}") for s in range(2)]
        xg_in = [sem(f"xg_in{s}") for s in range(2)]
        y_out = [sem(f"y_out{s}") for s in range(2)]
        yg_in = [sem(f"yg_in{s}") for s in range(2)]
        out_done = [sem(f"out_done{s}") for s in range(2)]
        gu_in = [sem(f"gu_in{k}") for k in range(KT)]
        dn_in = [sem(f"dn_in{k}") for k in range(KT)]

        def par_heads(m, par):
            return m.rearrange("p (k q) t -> p k q t", q=2)[:, :, par, :]

        def job_done(eng, job):
            eng.wait_ge(job_mm, JOB[job] + 1)

        def read_by(eng, job):
            if "A" in READERS[job[0]]:
                eng.wait_ge(act_read, reads_through("A", job))
            if "D" in READERS[job[0]]:
                eng.wait_ge(dve_read, reads_through("D", job))

        ada_blk = lambda b: ("ada", b)
        BLOCKS = [ada_blk(b) for b in range(4)] + [("w_in", 0), ("w_in", 512), ("w_in", COL_Q),
                  ("w_in", COL_K), ("w_in", COL_V), ("pf", 0)] + [ada_blk(b) for b in range(4, 12)]
        BLK_OF = {b: n for n, b in enumerate(BLOCKS)}
        LAST_JOB = [("ada", b) for b in range(4)] + [("rw", 3), ("rw", 7), ("q", 3), ("k", 3), ("v", 3),
                    ("f", 0)] + [("ada", b) for b in range(4, 12)]

        block = ctx.enter_context(nc.Block())

        @block.sync
        def _(sp):
            sp.dma_start(x_sb, a["x"][0].rearrange("(t p) d -> p t d", p=P)).then_inc(x_in, 16)
            ada_v = a["ada_w"][0].rearrange("(p k) n -> p k n", p=P)
            win_v = a["w_in"][0].rearrange("(k p) n -> p k n", p=P)
            for n, (kind, c) in enumerate(BLOCKS):
                if n >= 2:
                    job_done(sp, LAST_JOB[n - 2])
                elif n == 0:
                    sp.wait_ge(cst_dve, 1)
                dst = blk[n % 2]
                if kind == "ada":
                    sp.dma_start(dst, ada_v[:, :, 512 * c:512 * c + 512]).then_inc(blk_in[n % 2], 16)
                elif kind == "w_in":
                    sp.dma_start(dst, win_v[:, :, c:c + 512]).then_inc(blk_in[n % 2], 16)
                else:
                    sp.dma_start(dst[:, :, 0:256], win_v[:, :, COL_POOL:COL_POOL + 256]).then_inc(blk_in[n % 2], 16)
                    sp.dma_start(dst[:, :, 256:256 + FH], win_v[:, :, COL_F:COL_F + FH]).then_inc(blk_in[n % 2], 16)
            job_done(sp, ("trBK", TT - 1))
            sp.dma_start(x_sb, a["x"][0].rearrange("(t p) d -> p t d", p=P)).then_inc(x_in, 16)
            read_by(sp, ("QY", TT - 1))
            sp.dma_start(w_out_sb, a["w_out"][0].rearrange("(k p) n -> p k n", p=P)).then_inc(wout_in, 16)
            sp.wait_ge(fox_oe, 4)
            sp.dma_start(rw_sb, a["router_w"][0].rearrange("(k p) e -> p k e", p=P)).then_inc(small2_in, 16)
            sp.dma_start(rb, a["router_b"][0].partition_broadcast(P)).then_inc(small2_in, 16)
            sp.dma_start(braw[:, 0:2 * F], a["moe_b_gu"][0]).then_inc(small2_in, 16)
            sp.dma_start(braw[:, 2 * F:3 * F], a["moe_b_down"][0]).then_inc(small2_in, 16)
            sp.dma_start(norm2B, a["norm2"][0].partition_broadcast(P)).then_inc(small2_in, 16)

        def blk_ready(eng, b):
            n = BLK_OF[b]
            count = 16 * (n // 2 + 1)
            pf = BLK_OF[("pf", 0)]
            if n % 2 == pf % 2 and n >= pf:
                count += 16
            eng.wait_ge(blk_in[n % 2], count)

        @block.gpsimd
        def _(pool):
            n_chain = [0]

            def link(ins):
                n_chain[0] += 1
                ins.then_inc(pool_chain, 1)
                pool.wait_ge(pool_chain, n_chain[0])

            g = nc.gpsimd
            link(g.memset(ident[:], 0.0))
            link(g.affine_select(out=ident[:], in_=ident[:], compare_op=ALU.not_equal, fill=1.0, base=0,
                                 pattern=[[-1, P]], channel_multiplier=1))
            link(g.memset(strict[:], 0.0))
            link(g.affine_select(out=strict[:], in_=strict[:], compare_op=ALU.is_ge, fill=1.0, base=0,
                                 pattern=[[-1, P]], channel_multiplier=1))
            link(g.tensor_copy(strictb[:], strict[:]))
            link(g.memset(onesb[:], 1.0))
            link(g.memset(zeroE[:], 0.0))
            link(g.memset(zero_tab[:], 0))
            link(g.memset(bsel[:], 0.0))
            for part in range(3):
                link(g.affine_select(out=bsel[:], in_=bsel[:], compare_op=ALU.not_equal, fill=1.0, base=-E * part,
                                     pattern=[[-1, E]], channel_multiplier=1))
            link(g.iota(iotaE[:], pattern=[[1, E]], base=0, channel_multiplier=0,
                        allow_small_or_imprecise_dtypes=True))
            link(g.iota(iotaJ[:], pattern=[[1, MAXOV]], base=0, channel_multiplier=0,
                        allow_small_or_imprecise_dtypes=True))
            link(g.iota(tokid[:], pattern=[[P, TT]], base=0, channel_multiplier=1))
            link(g.iota(xi, pattern=[[0, P]], base=0, channel_multiplier=1))
            link(g.iota(yi, pattern=[[1, P]], base=0, channel_multiplier=0))
            link(g.memset(blockones[:], 0.0))
            for h in range(2):
                link(g.memset(blockones[HD * h:HD * h + HD, HD * h:HD * h + HD], 1.0))
            link(g.memset(causal[:], 0.0))
            link(g.affine_select(out=causal[:], in_=causal[:], compare_op=ALU.is_ge, fill=-1e30, base=0,
                                 pattern=[[-1, P]], channel_multiplier=1))
            link(g.memset(negsel[:], 0.0))
            link(g.affine_select(out=negsel[:], in_=negsel[:], compare_op=ALU.not_equal, fill=-1.0 / SM, base=0,
                                 pattern=[[-1, 8]], channel_multiplier=1))
            link(g.tensor_copy(identb[:], ident[:]))
            link(g.memset(scanmask[:], 1.0))
            link(g.memset(scanmask[:].rearrange("p (c s) -> p c s", s=CHUNK)[:, :, 0:1], 0.0))
            link(g.iota(rcnt[:], pattern=[[0, CT], [1, PAD]], base=1, channel_multiplier=0,
                        allow_small_or_imprecise_dtypes=True))
            link(g.memset(pz[:, :, 0:PAD], 0.0))
            g.memset(zraw[:, :, 0:1], 0.0).then_inc(cst_pool, 1)

            job_done(pool, ("f", 0))
            zero_src = Wt[:, 10240:10240 + D]
            link(g.memset(zero_src, 0.0))
            pool.dma_start(y_d[E * BLK:NB * BLK, :].rearrange("(b p) d -> p b d", p=P),
                           zero_src.unsqueeze(1).to_broadcast([P, MAXOV, D])).then_inc(y_zero, 16)
            for ct in range(CT):
                read_by(pool, ("pz", ct))
                if ct:
                    job_done(pool, ("pm", 0))
                z = pz[:, ct, :]
                n = S + PAD
                link(g.tensor_tensor(tA[:, 1:n], z[:, 1:n], z[:, 0:n - 1], ALU.add))
                last = g.tensor_tensor(tB[:, 3:n], tA[:, 3:n], tA[:, 1:n - 2], ALU.add)
                if ct:
                    link(last)
                    link(g.tensor_tensor(tA[:, 7:n], tB[:, 7:n], tB[:, 3:n - 4], ALU.add))
                    last = g.tensor_tensor(tB[:, 15:n], tA[:, 15:n], tA[:, 7:n - 8], ALU.add)
                last.then_inc(pool_sum, 1)
                if ct == 0:
                    for c2 in range(CT):
                        pool.wait_ge(kk_unit, c2 + 1)
                        link(g.tensor_tensor(aT[:, c2, :], Bh[:, c2, :], aT[:, c2, :], ALU.mult))
                        pool.wait_ge(exps, c2 + 1)
                        link(g.tensor_tensor(Bt[:, c2, :], aT[:, c2, :], Kt[:, c2, :], ALU.mult))
                        pool.wait_ge(elem_dve, 2 * c2 + 1)
                        g.tensor_tensor(Bh[:, c2, :], aT[:, c2, :], Kh[:, c2, :], ALU.mult).then_inc(elem_pool, 1)

            pool.wait_ge(shifted, 8)
            g.memset(ST[:, :, 0, :], 0.0).then_inc(st_zero, 1)
            bc = lambda m: m.unsqueeze(1).to_broadcast([P, RH, P])
            for q in range(2):
                for j in range(2):
                    t = 2 * q + j
                    read_by(pool, ("MP", t, 1))
                    read_by(pool, ("M", t, 1))
                    g.tensor_tensor(X[j], X[j], bc(ident[:]), ALU.add).then_inc(solve_pool, 1)
                    g.tensor_tensor(XT[j], XT[j], bc(ident[:]), ALU.add).then_inc(solve_pool, 1)
                    g.tensor_tensor(ML[j], MT[j], bc(lvl[:, 1, :]), ALU.mult).then_inc(solve_pool, 1)
                for lv in range(2, LEVELS):
                    for j in range(2):
                        job_done(pool, ("T", 2 * q + j, lv - 1))
                        g.tensor_tensor(ML[j], MT[j], bc(lvl[:, lv, :]), ALU.mult).then_inc(solve_pool, 1)

        PER_PAIR = 6 + 2 * (LEVELS - 2)

        def ml_count(t, lv):
            q, j = t // 2, t % 2
            return PER_PAIR * q + (3 * (j + 1) if lv == 1 else 6 + 2 * (lv - 2) + j + 1)

        @block.scalar
        def _(act):
            n_chain = [0]

            def link(ins):
                n_chain[0] += 1
                ins.then_inc(act_chain, 1)
                act.wait_ge(act_chain, n_chain[0])

            s = nc.scalar
            with nc.allow_non_contiguous_dma(reason="per-channel parameters, one column each"):
                act.dma_start(cT[:], a["c"].rearrange("o (p k) -> p (o k)", p=P)).then_inc(small_in, 16)
                for name, col, w in (("rwkv_mu", MU, 8), ("rwkv_w0", W0, 2), ("rwkv_a0", A0, 2),
                                     ("rwkv_k_k", KK_, 2), ("rwkv_k_a", KA, 2), ("rwkv_ln_w", LNW, 2),
                                     ("rwkv_ln_b", LNB, 2), ("pool_scale", PSC, 2)):
                    act.dma_start(cols[:, col:col + w], a[name].rearrange("o (c p) -> p (o c)", p=P)
                                  ).then_inc(small_in, 16)
                act.dma_start(cols[:, RK:RK + 2], a["rwkv_r_k"][0].rearrange("(c h) d -> (h d) c", c=CT)
                              ).then_inc(small_in, 16)
                act.dma_start(cols[0:FH, 24:25], a["fox_b_f"].rearrange("o f -> f o")).then_inc(small_in, 16)
            act.dma_start(up[0:HD, :], a["rwkv_w_up"][0]).then_inc(small_in, 16)
            act.dma_start(up[HD:P, :], a["rwkv_a_up"][0]).then_inc(small_in, 16)
            act.dma_start(g_up[:], a["rwkv_g_up"][0]).then_inc(small_in, 16)
            act.dma_start(pool_w[:], a["pool_w"][0].rearrange("(c h) i o -> (h i) c o", c=CT)).then_inc(small_in, 16)
            act.dma_start(norm1B, a["norm1"][0].partition_broadcast(P)).then_inc(bias_in, 16)
            act.dma_start(R[:, 0:6 * D], a["ada_b"][0].partition_broadcast(P)).then_inc(bias_in, 16)
            act.wait_ge(small_in, 16 * 15)
            s.activation(cs[:], cT[:], ACT.Sigmoid).then_inc(cond_sig, 1)
            act.wait_ge(x_in, 16)
            for t in range(TT):
                if t >= 2:
                    act.wait_ge(sq_done, t - 1)
                s.activation(htmp[:, t % 2, :], x_sb[:, t, :], ACT.Square,
                             accum_out=ss[:, t:t + 1]).then_inc(sq_done, 1)

            act.wait_ge(ms_rdy, 1)
            s.activation(rstd[:], rstd[:], ACT.Sqrt).then_inc(rms_rdy, 1)

            for step in STEPS:
                kind = step[0]
                if kind == "fox":
                    u = step[1]
                    if u < FH * TT:
                        n = P * (u % TT + 1)
                        act.wait_ge(fox_mx, u + 1)
                        if u >= 2:
                            act.wait_ge(fox_tr, u - 1)
                        s.activation(Pm[:, u % 2, 0:n], fox_s(u)[:, 0:n], ACT.Exp, scale=SM,
                                     bias=fmx[:, 4 * (u % 2) + 1:4 * (u % 2) + 2],
                                     accum_out=fmx[:, 4 * (u % 2) + 2:4 * (u % 2) + 3]).then_inc(fox_ex, 1)
                    v = u - 1
                    if 0 <= v < FH * TT and v % 2 == 0:
                        n = P * (v % TT + 1)
                        act.wait_ge(fox_tr, v + 1)
                        if v >= 2:
                            act.wait_ge(fox_pv, v - 1)
                        s.activation(PT[:, v % 2, 0:n], fox_t(v)[:, 0:n], ACT.Copy).then_inc(fox_pa, 1)
                    w = u - 2
                    if w >= 0 and w % (2 * TT) == 2 * TT - 1:
                        act.wait_ge(fox_pv, w + 1)
                        s.activation(fq[:, w // (2 * TT), :], fox_o, ACT.Copy).then_inc(fox_oe, 1)
                    continue
                if "A" not in READERS[kind]:
                    continue
                if kind == "lora" and step[1] == 0:
                    act.wait_ge(shifted, 7)
                    s.activation(WG[0:HD, 0, :], WG[0:HD, 0, :], ACT.Tanh).then_inc(lora_in, 1)
                    act.wait_ge(shifted, 8)
                    s.activation(WG[:, 1, :], WG[:, 1, :], ACT.Sigmoid).then_inc(lora_in, 1)
                if kind == "rw" and step[1] >= 2:
                    act.wait_ge(shifted, step[1] - 1)
                if kind == "kkn" and step[1] == 0:
                    for ct in range(CT):
                        act.wait_ge(kk_raw, ct + 1)
                        s.activation(Kh[:, ct, :], Bh[:, ct, :], ACT.Square).then_inc(kk_sq, 1)
                if kind == "pz" and step[1] == 0:
                    for ct in range(CT):
                        act.wait_ge(logs, ct + 1)
                        job_done(act, ("rk", ct))
                        s.activation(AR[:, ct, 1, :], L[:, ct, :], ACT.Exp)
                        s.activation(AR[:, ct, 0, :], AR[:, ct, 0, :], ACT.Exp)
                        s.activation(Kt[:, ct, :], L[:, ct, :], ACT.Exp, scale=-1.0)
                        s.activation(Kh[:, ct, :], Kh[:, ct, :], ACT.Exp)
                        s.activation(gam[:, ct, :], L[:, ct, :].rearrange("p (c s) -> p c s", s=CHUNK)[:, :, CHUNK - 1],
                                     ACT.Exp).then_inc(exps, 1)
                job_done(act, step)
                if "D" in READERS[kind]:
                    act.wait_ge(dve_read, reads_through("D", step))
                b = job_bank(step)
                if kind == "hT":
                    t, half = step[1], step[2]
                    ins = s.activation(hT[:, 4 * half:4 * half + 4, P * t:P * t + P],
                                       b.rearrange("p (k t) -> p k t", k=4), ACT.Copy)
                elif kind == "rw":
                    ins = s.activation(zraw[:, step[1] % 2, 1:S + 1], b, ACT.Copy)
                elif kind == "q":
                    ins = s.activation(fq[:, step[1], :], b, ACT.Copy)
                elif kind == "k":
                    ins = s.activation(fk[:, step[1], :], b, ACT.Copy)
                elif kind == "v":
                    ins = s.activation(fv[:, step[1], :], b, ACT.Copy)
                elif kind == "kkn":
                    act.wait_ge(rk_in, step[1] + 1)
                    ins = s.activation(AR[:, step[1], 0, :], b, ACT.Sqrt)
                elif kind == "lora":
                    what, ct = step[1] // 2, step[1] % 2
                    if what == 0:
                        ins = s.activation(Bt[:, ct, :], b, ACT.Sigmoid, bias=cols[:, W0 + ct:W0 + ct + 1])
                    elif what == 1:
                        ins = s.activation(aT[:, ct, :], b, ACT.Sigmoid, bias=cols[:, A0 + ct:A0 + ct + 1])
                    else:
                        ins = s.activation(gT[:, ct, :], b, ACT.Copy)
                elif kind == "pz":
                    ins = s.activation(pz[:, step[1], PAD:PAD + S], b, ACT.Copy)
                elif kind == "f":
                    ins = s.activation(fln[0:FH, :], b[0:FH, :], ACT.Abs, bias=cols[0:FH, 24:25])
                elif kind == "pm":
                    ct = step[1]
                    act.wait_ge(pooled, ct + 1)
                    ins = s.activation(pmix[:, ct, :], b, ACT.Copy, scale=cols[:, PSC + ct:PSC + ct + 1])
                elif kind == "trAV":
                    t = step[1]
                    ins = s.activation(Wt[:, 12288:14336].rearrange("p (w t c) -> p w t c", w=2, t=TT)[:, :, t, :],
                                       b.rearrange("p (w c) -> p w c", w=2), ACT.Copy)
                elif kind == "MP":
                    t, par = step[1], step[2]
                    if t >= 2:
                        act.wait_ge(solve_pool, PER_PAIR)
                    ins = s.activation(par_heads(MT[t % 2], par),
                                       b.rearrange("p (h w t) -> p h w t", h=2, w=2)[:, :, 0, :], ACT.Copy)
                elif kind == "T":
                    ins = s.activation(Tm[step[1] % 2], b.rearrange("p (h t) -> p h t", h=RH), ACT.Copy)
                elif kind == "NV":
                    ins = s.activation(Tm[step[1] % 2][:, :, 0:HD],
                                       b[:, 0:RW].rearrange("p (h v) -> p h v", h=RH), ACT.Copy)
                elif kind == "W":
                    ins = s.activation(ML[step[1] % 2], b.rearrange("p (h m) -> p h m", h=RH), ACT.Copy)
                elif kind == "QY":
                    t = step[1]
                    ins = s.activation(Yin[:, :, P * t:P * t + P],
                                       b.rearrange("p (c w t) -> p c w t", c=CT, w=2)[:, :, 1, :], ACT.Copy)
                elif kind == "GH":
                    t, cc = step[1], step[2]
                    act.wait_ge(y_zero, 16)
                    ins = s.activation(GH[:, :, 2 * t + cc, :], b[:, 0:RW].rearrange("p (x m) -> p x m", x=CT), ACT.Copy)
                ins.then_inc(act_read, 1)
                if kind == "f":
                    act.wait_ge(act_read, reads_through("A", step))
                    link(s.activation(fln[0:FH, :], fln[0:FH, :], ACT.Exp, scale=-1.0))
                    s.activation(fln[0:FH, :], fln[0:FH, :], ACT.Ln, bias=1.0).then_inc(f_ln, 1)

            for ct in range(CT):
                act.wait_ge(y_cen, ct + 1)
                s.activation(lnS[:, ct, :], lnC[:, ct, :], ACT.Square).then_inc(y_sq, 1)
            for ct in range(CT):
                act.wait_ge(var_rdy, ct + 1)
                s.activation(lnY[:, ct, :], lnY[:, ct, :], ACT.Sqrt).then_inc(std_rdy, 1)
            for ct in range(CT):
                act.wait_ge(y_scl, ct + 1)
                s.activation(lnC[:, ct, :], lnC[:, ct, :], ACT.Identity, scale=cols[:, LNW + ct:LNW + ct + 1],
                             bias=cols[:, LNB + ct:LNB + ct + 1]).then_inc(y_aff, 1)

        @block.vector
        def _(dve):
            n_chain = [0]

            def link(ins):
                n_chain[0] += 1
                ins.then_inc(dve_chain, 1)
                dve.wait_ge(dve_chain, n_chain[0])

            v = nc.vector
            dve.wait_ge(cst_pool, 1)
            link(v.tensor_tensor(xi, xi, yi, ALU.bitwise_xor))
            xf = Wt[:, 2 * P:3 * P]
            link(v.tensor_copy(xf, xi))
            ge = [Wt[:, (3 + n) * P:(4 + n) * P] for n in range(LEVELS + 1)]
            for n in range(LEVELS + 1):
                link(v.scalar_tensor_tensor(out=ge[n], in0=xf, scalar=float(1 << n), in1=strict[:],
                                            op0=ALU.is_ge, op1=ALU.mult))
            for n in range(LEVELS):
                link(v.tensor_tensor(lvl[:, n, :], ge[n], ge[n + 1], ALU.subtract))
            link(v.tensor_tensor(strict[:], strict[:], ge[LEVELS], ALU.subtract))
            link(v.tensor_tensor(incl[:], strict[:], ident[:], ALU.add))
            link(v.tensor_scalar(lvl0T[:], xf, 1.0, None, ALU.is_equal))
            link(v.tensor_tensor(lvl0T[:], lvl0T[:], lvl[:, 0, :], ALU.subtract))
            for ct in range(CT):
                for h in range(2):
                    w = float(POOL_WINDOWS[2 * ct + h])
                    link(v.tensor_scalar(rcnt[HD * h:HD * h + HD, ct, :], rcnt[HD * h:HD * h + HD, ct, :], w, None, ALU.min))
            link(v.reciprocal(rcnt[:], rcnt[:]))
            v.memset(stmp[:], 0.0).then_inc(cst_dve, 1)
            dve.wait_ge(cond_sig, 1)
            link(v.tensor_tensor(cs[:], cs[:], cT[:], ALU.mult))
            v.tensor_copy(condB, cs[:].unsqueeze(2).to_broadcast([P, KT, P])).then_inc(cond_rdy, 1)
            dve.wait_ge(sq_done, TT)
            v.tensor_scalar(rstd[:], ss[:], 1.0 / D, NORM_EPS, ALU.mult, ALU.add).then_inc(ms_rdy, 1)
            dve.wait_ge(rms_rdy, 1)
            link(v.reciprocal(rstd[:], rstd[:]))

            z_dest = [rT[:, 0, :], rT[:, 1, :], kT[:, 0, :], kT[:, 1, :], vT[:, 0, :], vT[:, 1, :],
                      WG[:, 0, :], WG[:, 1, :]]
            bc2 = lambda m: m.unsqueeze(1).to_broadcast([P, 2, P])
            for step in STEPS:
                kind = step[0]
                if kind == "fox":
                    u = step[1]
                    if u < FH * TT:
                        n = P * (u % TT + 1)
                        dve.wait_ge(fox_sc, u + 1)
                        m = fmx[:, 4 * (u % 2):4 * (u % 2) + 4]
                        link(v.reduce_max(m[:, 0:1], fox_s(u)[:, 0:n], AX_X))
                        v.tensor_scalar(m[:, 1:2], m[:, 0:1], -SM, None, ALU.mult).then_inc(fox_mx, 1)
                    w = u - 1
                    if 0 <= w < FH * TT:
                        n = P * (w % TT + 1)
                        m = fmx[:, 4 * (w % 2):4 * (w % 2) + 4]
                        dve.wait_ge(fox_ex, w + 1)
                        link(v.reciprocal(m[:, 3:4], m[:, 2:3]))
                        v.tensor_scalar(Pm[:, w % 2, 0:n], Pm[:, w % 2, 0:n], m[:, 3:4], None,
                                        ALU.mult).then_inc(fox_nm, 1)
                        if w % 2:
                            dve.wait_ge(fox_tr, w + 1)
                            if w >= 2:
                                dve.wait_ge(fox_pv, w - 1)
                            v.tensor_copy(PT[:, w % 2, 0:n], fox_t(w)[:, 0:n]).then_inc(fox_pd, 1)
                    continue
                if kind == "hT" and step[2] == 0:
                    t = step[1]
                    if t == 0:
                        dve.wait_ge(dve_read, 4)
                        link(v.scalar_tensor_tensor(out=mod[:, 1, :], in0=mod[:, 1, :], scalar=1.0, in1=norm1B,
                                                    op0=ALU.add, op1=ALU.mult))
                    if t >= 2:
                        job_done(dve, ("hT", t - 2, 1))
                    h = htmp[:, t % 2, :]
                    link(v.scalar_tensor_tensor(out=h, in0=x_sb[:, t, :], scalar=rstd[:, t:t + 1],
                                                in1=mod[:, 1, :], op0=ALU.mult, op1=ALU.mult))
                    v.tensor_tensor(h, h, mod[:, 0, :], ALU.add).then_inc(h_add, 1)
                if kind == "rw":
                    n = step[1]
                    read_by(dve, step)
                    zr = zraw[:, n % 2, :]
                    d = z_dest[n]
                    link(v.tensor_tensor(d, zr[:, 0:S], zr[:, 1:S + 1], ALU.subtract))
                    v.scalar_tensor_tensor(out=d, in0=d, scalar=cols[:, MU + n:MU + n + 1], in1=zr[:, 1:S + 1],
                                           op0=ALU.mult, op1=ALU.add).then_inc(shifted, 1)
                if kind == "q" and step[1] == 0:
                    dve.wait_ge(shifted, 8)
                    for ct in range(CT):
                        v.tensor_scalar(Bh[:, ct, :], kT[:, ct, :], cols[:, KK_ + ct:KK_ + ct + 1], None,
                                        ALU.mult).then_inc(kk_raw, 1)
                if kind == "k" and step[1] == 0:
                    for ct in range(CT):
                        read_by(dve, ("lora", 2 + ct))
                        link(v.tensor_scalar(AR[:, ct, 0, :], aT[:, ct, :], 1.0, cols[:, KA + ct:KA + ct + 1],
                                             ALU.subtract, ALU.mult))
                        dve.wait_ge(kk_raw, ct + 1)
                        link(v.scalar_tensor_tensor(out=kT[:, ct, :], in0=AR[:, ct, 0, :], scalar=1.0,
                                                    in1=kT[:, ct, :], op0=ALU.add, op1=ALU.mult))
                        v.scalar_tensor_tensor(out=AR[:, ct, 1, :], in0=rT[:, ct, :],
                                               scalar=cols[:, RK + ct:RK + ct + 1], in1=kT[:, ct, :],
                                               op0=ALU.mult, op1=ALU.mult).then_inc(rk_in, 1)
                    for ct in range(CT):
                        link(v.tensor_scalar(Bt[:, ct, :], Bt[:, ct, :], DECAY, None, ALU.mult))
                        link(v.tensor_tensor_scan(out=L[:, ct, :], data0=scanmask[:], data1=Bt[:, ct, :], initial=0.0,
                                                  op0=ALU.mult, op1=ALU.add))
                if kind == "kkn":
                    ct = step[1]
                    read_by(dve, step)
                    link(v.tensor_scalar(AR[:, ct, 0, :], AR[:, ct, 0, :], 1e-12, None, ALU.max))
                    link(v.reciprocal(AR[:, ct, 0, :], AR[:, ct, 0, :]))
                    v.tensor_tensor(Bh[:, ct, :], Bh[:, ct, :], AR[:, ct, 0, :], ALU.mult).then_inc(kk_unit, 1)
                    dve.wait_ge(kk_unit, ct + 1)
                    link(v.tensor_tensor(AR[:, ct, 0, :], L[:, ct, :], Bt[:, ct, :], ALU.subtract))
                    Lc = L[:, ct, :].rearrange("p (c s) -> p c s", s=CHUNK)
                    v.tensor_tensor(Kh[:, ct, :].rearrange("p (c s) -> p c s", s=CHUNK),
                                    Lc[:, :, CHUNK - 1:CHUNK].to_broadcast([P, NC, CHUNK]), Lc,
                                    ALU.subtract).then_inc(logs, 1)
                if "D" not in READERS[kind]:
                    continue
                job_done(dve, step)
                b = job_bank(step)
                if kind == "ada":
                    n = step[1]
                    dve.wait_ge(bias_in, 32)
                    m = R[:, 512 * n:512 * n + 512]
                    ins = v.tensor_tensor(m, b, m, ALU.add)
                elif kind == "rk":
                    ct = step[1]
                    ins = v.tensor_tensor(rkv[:, ct, :], b, vT[:, ct, :], ALU.mult)
                elif kind == "f":
                    ins = v.tensor_scalar(fmin[0:FH, :], b[0:FH, :], cols[0:FH, 24:25], 0.0, ALU.add, ALU.min)
                elif kind == "trBK":
                    t = step[1]
                    ins = v.tensor_copy(Wt[:, 14336:16384].rearrange("p (w t c) -> p w t c", w=2, t=TT)[:, :, t, :],
                                        b.rearrange("p (w c) -> p w c", w=2))
                elif kind == "MP":
                    t, par = step[1], step[2]
                    j = t % 2
                    bv = b.rearrange("p (h w t) -> p h w t", h=2, w=2)
                    v.tensor_tensor(par_heads(XT[j], par), bv[:, :, 0, :], bc2(lvl[:, 0, :]), ALU.mult)
                    ins = v.tensor_tensor(par_heads(PbT[j], par), bv[:, :, 1, :], bc2(incl[:]), ALU.mult)
                elif kind == "M":
                    ins = v.tensor_tensor(par_heads(X[step[1] % 2], step[2]),
                                          b[:, 0:RW].rearrange("p (h t) -> p h t", h=2), bc2(lvl0T[:]), ALU.mult)
                elif kind == "NP":
                    t, par = step[1], step[2]
                    j = t % 2
                    bv = b.rearrange("p (h w t) -> p h w t", h=2, w=2)
                    v.tensor_tensor(par_heads(NT[j], par), bv[:, :, 0, :], bc2(strict[:]), ALU.mult)
                    ins = v.tensor_tensor(par_heads(PkT[j], par), bv[:, :, 1, :], bc2(incl[:]), ALU.mult)
                elif kind == "XA":
                    j = step[1] % 2
                    ins = v.tensor_tensor(X[j], b.rearrange("p (h t) -> p h t", h=RH), X[j], ALU.add)
                elif kind == "XB":
                    j = step[1] % 2
                    ins = v.tensor_tensor(XT[j], b.rearrange("p (h t) -> p h t", h=RH), XT[j], ALU.add)
                elif kind == "QY":
                    t = step[1]
                    ts = slice(P * t, P * t + P)
                    ins = v.tensor_tensor(QT[:, :, ts], b.rearrange("p (c w t) -> p c w t", c=CT, w=2)[:, :, 0, :],
                                          AR[:, :, 1, ts], ALU.add)
                ins.then_inc(dve_read, 1)
                if kind == "f":
                    dve.wait_ge(f_ln, 1)
                    dve.wait_ge(dve_read, reads_through("D", step))
                    v.tensor_tensor_scan(out=cum[0:FH, :], data0=fmin[0:FH, :], data1=fln[0:FH, :], initial=0.0,
                                         op0=ALU.add, op1=ALU.subtract).then_inc(cum_rdy, 1)
                    for ct in range(CT):
                        dve.wait_ge(exps, ct + 1)
                        v.scalar_tensor_tensor(out=AR[:, ct, 0, :], in0=Bh[:, ct, :], scalar=-1.0,
                                               in1=AR[:, ct, 0, :], op0=ALU.mult, op1=ALU.mult).then_inc(elem_dve, 1)
                        v.tensor_tensor(AR[:, ct, 1, :], rT[:, ct, :], AR[:, ct, 1, :], ALU.mult)
                        dve.wait_ge(elem_pool, ct + 1)
                        v.tensor_tensor(Kt[:, ct, :], kT[:, ct, :], Kt[:, ct, :], ALU.mult)
                        v.tensor_tensor(Kh[:, ct, :], kT[:, ct, :], Kh[:, ct, :], ALU.mult).then_inc(elem_dve, 1)
                if step in (("ada", 7), ("trBK", TT - 1)):
                    ct = ("ada", "trBK").index(kind)
                    dve.wait_ge(pool_sum, ct + 1)
                    for h in range(2):
                        hs = slice(HD * h, HD * h + HD)
                        tt = (tA, tB)[h][hs, :]
                        link(v.tensor_tensor(fix[hs, :], tt[:, PAD:2 * PAD], rcnt[hs, ct, :], ALU.mult))
                        link(v.tensor_tensor(fix[hs, :], fix[hs, :], pz[hs, ct, PAD:2 * PAD], ALU.subtract))
                        link(v.scalar_tensor_tensor(out=tt[:, PAD:PAD + S], in0=tt[:, PAD:PAD + S],
                                                    scalar=1.0 / POOL_WINDOWS[2 * ct + h], in1=pz[hs, ct, PAD:PAD + S],
                                                    op0=ALU.mult, op1=ALU.subtract))
                        last = v.tensor_copy(tt[:, PAD:2 * PAD], fix[hs, :])
                        if h == 0:
                            link(last)
                    last.then_inc(pooled, 1)

            dve.wait_ge(st_zero, 1)
            read_by(dve, ("GH", TT - 1, 1))
            for c in range(NC - 1):
                if c:
                    dve.wait_ge(st_new, c)
                for ct in range(CT):
                    ins = v.scalar_tensor_tensor(out=stmp[:, ct, :], in0=ST[:, ct, c, :], scalar=gam[:, ct, c:c + 1],
                                                 in1=GH[:, ct, c, HD:P], op0=ALU.mult, op1=ALU.add)
                link(ins)
                dve.wait_ge(st_mm, c + 1)
                v.tensor_tensor(ST[:, :, c + 1, :], ps[:, 5, 0:P].rearrange("p (x v) -> p x v", x=CT), stmp[:],
                                ALU.add).then_inc(st_new, 1)
            for ct in range(CT):
                dve.wait_ge(y_mm, 1)
                v.tensor_tensor(lnY[:, ct, :], ps[:, 3 + ct, :], Yin[:, ct, :], ALU.add).then_inc(y_sum, 1)
            for ct in range(CT):
                dve.wait_ge(mean_mm, ct + 1)
                v.scalar_tensor_tensor(out=lnC[:, ct, :], in0=ps[:, 6 + ct, :], scalar=-1.0 / HD, in1=lnY[:, ct, :],
                                       op0=ALU.mult, op1=ALU.add).then_inc(y_cen, 1)
            for ct in range(CT):
                dve.wait_ge(var_mm, ct + 1)
                v.tensor_scalar(lnY[:, ct, :], ps[:, 3 + ct, :], 1.0 / HD, GN_EPS, ALU.mult, ALU.add).then_inc(var_rdy, 1)
                dve.wait_ge(std_rdy, ct + 1)
                link(v.reciprocal(lnY[:, ct, :], lnY[:, ct, :]))
                v.tensor_tensor(lnC[:, ct, :], lnC[:, ct, :], lnY[:, ct, :], ALU.mult).then_inc(y_scl, 1)
            for ct in range(CT):
                dve.wait_ge(y_aff, ct + 1)
                link(v.tensor_tensor(rkv[:, ct, :], lnC[:, ct, :], rkv[:, ct, :], ALU.add))
                v.tensor_tensor(rkv[:, ct, :], rkv[:, ct, :], gT[:, ct, :], ALU.mult).then_inc(rw_out, 1)

        @block.tensor
        def _(pe):
            mm = nc.tensor.matmul

            def head(h):
                return HD * (h % 2), h // 2

            pe.wait_ge(cond_rdy, 1)
            pe.wait_ge(cst_dve, 1)
            for step in STEPS:
                kind = step[0]
                if kind == "fox":
                    u = step[1]
                    if u < FH * TT:
                        h, i = u // TT, u % TT
                        po, ct = head(h)
                        n = P * (i + 1)
                        if u == 0:
                            pe.wait_ge(cum_rdy, 1)
                            read_by(pe, ("v", TT - 1))
                        if u >= 2:
                            pe.wait_ge(fox_ex, u - 1)
                        o = fox_s(u)[:, 0:n]
                        mm(o, fq[po:po + HD, ct, P * i:P * i + P], fk[po:po + HD, ct, 0:n], start=True, stop=False)
                        mm(o, negsel[:, h:h + 1].to_broadcast([8, P]), cum[0:FH, 0:n], start=False, stop=False)
                        mm(o[:, n - P:n], identb[:], causal[:], start=False, stop=True).then_inc(fox_sc, 1)
                    w = u - 1
                    if 0 <= w < FH * TT:
                        pe.wait_ge(fox_nm, w + 1)
                        if w >= 2:
                            pe.wait_ge(fox_pd if w % 2 else fox_pa, w // 2)
                        for kt in range(w % TT + 1):
                            ins = nc.tensor.transpose(fox_t(w)[:, P * kt:P * kt + P],
                                                      Pm[:, w % 2, P * kt:P * kt + P], ident[:])
                        ins.then_inc(fox_tr, 1)
                    w = u - 2
                    if 0 <= w < FH * TT:
                        h, i = w // TT, w % TT
                        po, ct = head(h)
                        pe.wait_ge(fox_pd if w % 2 else fox_pa, w // 2 + 1)
                        if ct and w % (2 * TT) == 0:
                            pe.wait_ge(fox_oe, ct)
                        for kt in range(i + 1):
                            ins = mm(fox_o[po:po + HD, P * i:P * i + P], fv[:, kt, HD * h:HD * h + HD],
                                     PT[:, w % 2, P * kt:P * kt + P], start=(kt == 0), stop=(kt == i))
                        ins.then_inc(fox_pv, 1)
                    continue
                n = JOB[step]
                if n >= JOB_BANKS:
                    read_by(pe, JOBS[n - JOB_BANKS])
                b = job_bank(step)
                if kind == "ada":
                    c = step[1]
                    blk_ready(pe, ("ada", c))
                    w = blk[BLK_OF[("ada", c)] % 2]
                    for k in range(KT):
                        ins = mm(b, condB[:, k, :], w[:, k, :], start=(k == 0), stop=(k == KT - 1))
                elif kind == "hT":
                    t, half = step[1], step[2]
                    pe.wait_ge(h_add, t + 1)
                    for k in range(4):
                        ins = nc.tensor.transpose(b[:, P * k:P * k + P],
                                                  htmp[:, t % 2, P * (4 * half + k):P * (4 * half + k) + P], ident[:])
                elif kind in ("rw", "q", "k", "pz", "f"):
                    m = step[1]
                    if kind == "rw":
                        key, c = ("w_in", 512 * (m // 4)), P * (m % 4)
                        if m == 0:
                            read_by(pe, ("hT", TT - 1, 1))
                    elif kind in ("q", "k"):
                        key, c = ("w_in", COL_Q if kind == "q" else COL_K), P * m
                    else:
                        key, c = ("pf", 0), (P * m if kind == "pz" else 2 * P)
                    rows = FH if kind == "f" else P
                    blk_ready(pe, key)
                    w = blk[BLK_OF[key] % 2]
                    for k in range(KT):
                        ins = mm(b[0:rows, :], w[:, k, c:c + rows], hT[:, k, :], start=(k == 0), stop=(k == KT - 1))
                elif kind == "v":
                    t = step[1]
                    blk_ready(pe, ("w_in", COL_V))
                    w = blk[BLK_OF[("w_in", COL_V)] % 2]
                    for k in range(KT):
                        ins = mm(b, hT[:, k, P * t:P * t + P], w[:, k, :], start=(k == 0), stop=(k == KT - 1))
                elif kind == "lora":
                    what, ct = step[1] // 2, step[1] % 2
                    cs_ = slice(P * ct, P * ct + P)
                    pe.wait_ge(lora_in, 2)
                    if what == 0:
                        ins = mm(b, up[0:HD, cs_], WG[0:HD, 0, :], start=True, stop=True)
                    elif what == 1:
                        ins = mm(b, up[HD:P, cs_], WG[HD:P, 0, :], start=True, stop=True)
                    else:
                        ins = mm(b, g_up[:, cs_], WG[:, 1, :], start=True, stop=True)
                elif kind == "kkn":
                    pe.wait_ge(kk_sq, step[1] + 1)
                    ins = mm(b, blockones[:], Kh[:, step[1], :], start=True, stop=True)
                elif kind == "rk":
                    pe.wait_ge(rk_in, step[1] + 1)
                    ins = mm(b, blockones[:], AR[:, step[1], 1, :], start=True, stop=True)
                elif kind == "pm":
                    ct = step[1]
                    pe.wait_ge(pooled, ct + 1)
                    for h in range(2):
                        hs = slice(HD * h, HD * h + HD)
                        ins = mm(b[hs, :], pool_w[hs, ct, :], (tA, tB)[h][hs, PAD:PAD + S], start=True, stop=True)
                elif kind in ("trAV", "trBK"):
                    t = step[1]
                    ts = slice(P * t, P * t + P)
                    pe.wait_ge(elem_dve, 2 * CT)
                    pe.wait_ge(elem_pool, CT)
                    for w in range(2):
                        for ct in range(CT):
                            if kind == "trAV":
                                src = (AR[:, ct, 0, ts], vT[:, ct, ts])[w]
                            else:
                                src = (Bh[:, ct, ts], Kh[:, ct, ts])[w]
                            ins = nc.tensor.transpose(b[:, RW * w + P * ct:RW * w + P * ct + P], src, ident[:])
                else:
                    t = step[1]
                    j = t % 2
                    ts = slice(P * t, P * t + P)
                    if kind in ("MP", "NP"):
                        if t % 2 == 0 and kind == "MP" and step[2] == 0:
                            job_done(pe, ("ada", 11))
                        for hh in range(2):
                            po, ct = head(2 * hh + step[2])
                            ins = mm(b[:, RW * hh:RW * hh + RW].rearrange("p (w t) -> p w t", w=2),
                                     (Bt if kind == "MP" else Kt)[po:po + HD, ct, ts], AR[po:po + HD, ct, :, ts],
                                     start=True, stop=True)
                    elif kind == "M":
                        for hh in range(2):
                            po, ct = head(2 * hh + step[2])
                            ins = mm(b[:, P * hh:P * hh + P], AR[po:po + HD, ct, 0, ts], Bt[po:po + HD, ct, ts],
                                     start=True, stop=True)
                    elif kind == "T":
                        lv = step[2]
                        pe.wait_ge(solve_pool, ml_count(t, lv))
                        if lv > 1:
                            read_by(pe, ("XA", t, lv - 1))
                        for h in range(RH):
                            ins = mm(b[:, P * h:P * h + P], ML[j][:, h, :], X[j][:, h, :], start=True, stop=True)
                    elif kind in ("XA", "XB"):
                        lv = step[2]
                        read_by(pe, ("T", t, lv))
                        if lv > 1:
                            read_by(pe, ("XB", t, lv - 1))
                        for h in range(RH):
                            lhs, rhs = (XT, Tm) if kind == "XA" else (Tm, XT)
                            ins = mm(b[:, P * h:P * h + P], lhs[j][:, h, :], rhs[j][:, h, :], start=True, stop=True)
                    elif kind == "NV":
                        read_by(pe, ("NP", t, 1))
                        for h in range(RH):
                            ins = mm(b[:, HD * h:HD * h + HD], NT[j][:, h, :], tokV[:, t, HD * h:HD * h + HD],
                                     start=True, stop=True)
                    elif kind == "W":
                        read_by(pe, ("NV", t))
                        read_by(pe, ("XB", t, LEVELS - 1))
                        for h in range(RH):
                            o = b[:, P * h:P * h + P]
                            mm(o[:, 0:HD], XT[j][:, h, :], tokA[:, t, HD * h:HD * h + HD], start=True, stop=True)
                            ins = mm(o[:, HD:P], XT[j][:, h, :], Tm[j][:, h, 0:HD], start=True, stop=True)
                    elif kind == "QY":
                        read_by(pe, ("W", t))
                        read_by(pe, ("NP", t, 1))
                        for h in range(RH):
                            po, ct = head(h)
                            o = b[po:po + HD, RW * ct:RW * ct + RW]
                            mm(o[:, 0:P], W12[j][:, h, 0, :], PbT[j][:, h, :], start=True, stop=True)
                            mm(o[:, P:2 * P], W12[j][:, h, 1, :], PbT[j][:, h, :], start=True, stop=False)
                            ins = mm(o[:, P:2 * P], tokV[:, t, HD * h:HD * h + HD], PkT[j][:, h, :],
                                     start=False, stop=True)
                    elif kind == "GH":
                        for h in range(RH):
                            po, ct = head(h)
                            hc = slice(HD * h, HD * h + HD)
                            rs = slice(CHUNK * step[2], CHUNK * step[2] + CHUNK)
                            o = b[po:po + HD, P * ct:P * ct + P]
                            mm(o[:, 0:HD], W12[j][rs, h, 0, :], tokB[rs, t, hc], start=True, stop=True)
                            mm(o[:, HD:P], tokB[rs, t, hc], W12[j][rs, h, 1, :], start=True, stop=False)
                            ins = mm(o[:, HD:P], tokK[rs, t, hc], tokV[rs, t, hc], start=False, stop=True)
                ins.then_inc(job_mm, 1)

            read_by(pe, ("GH", TT - 1, 1))
            read_by(pe, ("QY", TT - 1))
            pe.wait_ge(fox_oe, 4)
            pe.wait_ge(st_zero, 1)
            for c in range(NC):
                if c:
                    pe.wait_ge(st_new, c)
                if c < NC - 1:
                    for h in range(RH):
                        po, ct = head(h)
                        ins = mm(ps[po:po + HD, 5, HD * ct:HD * ct + HD], GH[po:po + HD, ct, c, 0:HD],
                                 ST[po:po + HD, ct, c, :], start=True, stop=True)
                    ins.then_inc(st_mm, 1)
                for h in range(RH):
                    po, ct = head(h)
                    ins = mm(ps[po:po + HD, 3 + ct, CHUNK * c:CHUNK * c + CHUNK], ST[po:po + HD, ct, c, :],
                             QT[po:po + HD, ct, CHUNK * c:CHUNK * c + CHUNK], start=True, stop=True)
            ins.then_inc(y_mm, 1)
            for ct in range(CT):
                pe.wait_ge(y_sum, ct + 1)
                mm(ps[:, 6 + ct, :], blockones[:], lnY[:, ct, :], start=True, stop=True).then_inc(mean_mm, 1)
            for ct in range(CT):
                pe.wait_ge(y_sq, ct + 1)
                mm(ps[:, 3 + ct, :], blockones[:], lnS[:, ct, :], start=True, stop=True).then_inc(var_mm, 1)
        x2 = x_sb
        h2 = [R[:, 11264:12288], R[:, 12288:13312]]
        h2T = R[:, 13312:14336].rearrange("p (k t) -> p k t", k=KT)
        xg = [R[:, 0:1024], R[:, 1024:2048]]
        xT = [R3(2048 + 1024 * s, KT, BLK) for s in range(2)]
        actv = R[:, 4096:5120]
        gate_b, sig_b, up_b = R[:, 11264:12288], R[:, 12288:13312], R[:, 13312:14336]
        aTr = R3(14336, F // P, BLK)
        ysb = [R[:, 15360:16384], R[:, 16384:17408]]
        bparts = R[:, 20480:22016].bitcast(BF16)
        btmp = R[0:E, 22016:22528].bitcast(BF16)
        normfB = R[:, 23584:24608]
        yg = [[R[:, 1024 * k:1024 * k + 1024] for k in range(TOPK)],
              [R[:, 11264 + 1024 * k:12288 + 1024 * k] for k in range(TOPK)]]
        comb = ysb
        w_gu_sb = W3(0, KT, 2 * F)
        w_dn_sb = W3(16384, F // P, D)

        mixed = [rkv[:, 0, :], rkv[:, 1, :], pmix[:, 0, :], pmix[:, 1, :]] + [fq[:, m, :] for m in range(4)]


        def load_experts(sp, n_gu, e_gu, n_dn, e_dn):
            gu_v = a["moe_w_gu"][0].rearrange("e k n -> (e k) n")
            dn_v = a["moe_w_down"][0].rearrange("e k n -> (e k) n")
            if e_gu is not None:
                for k in range(KT):
                    if n_gu is not None:
                        sp.wait_ge(gu_used, KT * (n_gu - 1) + k + 1)
                    sp.dma_start(w_gu_sb[:, k, :], gu_v[bass.ds(e_gu * D + P * k, P), :]).then_inc(gu_in[k], 16)
            if e_dn is not None:
                for k in range(KT):
                    if n_dn is not None:
                        sp.wait_ge(dn_used, KT * (n_dn - 1) + k + 1)
                    sp.dma_start(w_dn_sb[:, k, :], dn_v[bass.ds(e_dn * F + P * k, P), :]).then_inc(dn_in[k], 16)

        def overflow_count(eng):
            eng.wait_ge(ov_rdy, 1)
            return eng.value_load(ovI[0:1, NB - E:NB - E + 1], min_val=0, max_val=MAXOV)

        @block.sync
        def _(sp):
            rw_free = rw_out
            sp.wait_ge(rw_free, 2)
            load_experts(sp, None, 0, None, None)
            sp.dma_start(normfB, a["norm_f"].partition_broadcast(P)).then_inc(normf_in, 16)
            sp.wait_ge(p_mm, TT)
            load_experts(sp, None, None, None, 0)
            load_experts(sp, 1, 1, None, None)
            with sp.Fori(2, E) as n:
                load_experts(sp, n, n, n - 1, n - 1)
            load_experts(sp, None, None, E - 1, E - 1)
            ov = overflow_count(sp)
            with sp.If(ov > 0):
                with sp.Fori(0, ov) as j:
                    e = sp.value_load(ovI[0:1, bass.ds(j, 1)], min_val=0, max_val=E - 1)
                    load_experts(sp, E + j, e, E + j, e)

        @block.gpsimd
        def _(pool):
            def carry(c):
                nc.gpsimd.tensor_tensor(carried[:, c:c + 1], iotaE[:, 0:1], iotaE[:, 0:1], ALU.add)

            def gather(n, s, lag):
                if lag is not None:
                    pool.wait_ge(xt_mm, n - lag)
                    carry(0)
                nc.gpsimd.tensor_copy(icol[s][:], tok[:, bass.ds(n, 1)]).then_inc(ic_rdy, 1)
                pool.wait_ge(ic_rdy, n + 1)
                carry(1)
                nc.gpsimd.indirect_dma_start(out=xg[s], out_offset=None, in_=h2_d,
                                             in_offset=bass.IndirectOffsetOnAxis(ap=icol[s][:, 0:1], axis=0)
                                             ).then_inc(xg_in[s], 16)

            pool.dma_start(tab_d.rearrange("(p b) o -> p (b o)", p=P), zero_tab[:]).then_inc(tab_zero, 16)
            pool.wait_ge(slots_rdy, 1)
            pool.wait_ge(tab_zero, 16)
            for t in range(TT):
                for k in range(TOPK):
                    m = TOPK * t + k
                    nc.gpsimd.indirect_dma_start(out=tab_d, out_offset=bass.IndirectOffsetOnAxis(ap=tabI[:, m:m + 1], axis=0),
                                                 in_=tokid[:, t:t + 1], in_offset=None).then_inc(scat, 16)
            pool.wait_ge(scat, 16 * TT * TOPK)
            pool.dma_start(tok[:], tab_d.rearrange("(p b) o -> p (b o)", p=P)).then_inc(tok_in, 16)
            pool.wait_ge(tok_in, 16)
            for s in range(2):
                pool.wait_ge(h2_out[s], 16 * TT // 2)
            gather(0, 0, None)
            gather(1, 1, None)
            with pool.Fori(1, E // 2) as m:
                for s in range(2):
                    gather(2 * m + s, s, 1)
            ov = overflow_count(pool)
            with pool.If(ov > 0):
                with pool.Fori(0, ov) as j:
                    gather(E + j, 0, 0)
            pool.wait_ge(at_mm, E + ov)
            pool.wait_ge(y_out[0], 16 * (E // 2) + 16 * ov)
            pool.wait_ge(y_out[1], 16 * (E // 2))
            carry(0)
            for t in range(TT):
                if t >= 2:
                    pool.wait_ge(comb_done, t - 1)
                for k in range(TOPK):
                    m = TOPK * t + k
                    nc.gpsimd.indirect_dma_start(out=yg[t % 2][k], out_offset=None, in_=y_d,
                                                 in_offset=bass.IndirectOffsetOnAxis(ap=slotI[:, m:m + 1], axis=0)
                                                 ).then_inc(yg_in[t % 2], 16)
            for s in range(2):
                pool.wait_ge(out_done[s], 32)

        @block.scalar
        def _(act):
            s_ = nc.scalar
            act.wait_ge(small2_in, 16 * 5)
            for t in range(TT):
                act.wait_ge(x2_rdy, t + 1)
                s_.activation(h2[t % 2], x2[:, t, :], ACT.Square, accum_out=ss[:, t:t + 1]).then_inc(sq2_done, 1)
                act.wait_ge(ms2_rdy, t + 1)
                s_.activation(rstd[:, t:t + 1], rstd[:, t:t + 1], ACT.Sqrt).then_inc(rms2_rdy, 1)
                act.wait_ge(h2_rdy, t + 1)
                act.dma_start(h2_d[P * t:P * t + P, :], h2[t % 2]).then_inc(h2_out[t % 2], 16)
                act.wait_ge(h2t_mm, t + 1)
                if t:
                    act.wait_ge(lg_mm, t)
                s_.activation(h2T, ps[:, 4:6, :].rearrange("p b (k t) -> p (b k) t", k=4), ACT.Copy).then_inc(h2t_ev, 1)
            act.wait_ge(gdif_rdy, 1)
            s_.activation(gates[:], gates[:], ACT.Exp).then_inc(gexp_rdy, 1)

            def xt_evac(n, s, lag):
                act.wait_ge(xt_mm, n + 1)
                if lag is not None:
                    act.wait_ge(gu_used, KT * (n - lag))
                s_.activation(xT[s], ps[:, 4:6, :].rearrange("p b (k t) -> p (b k) t", k=4), ACT.Copy).then_inc(xt_ev, 1)

            def at_evac(n, first):
                act.wait_ge(at_mm, n + 1)
                if not first:
                    act.wait_ge(dn_used, KT * n)
                s_.activation(aTr, ps[:, 4:6, :].rearrange("p b (k t) -> p (b k) t", k=4), ACT.Copy).then_inc(at_ev, 1)

            def sigmoid(n):
                act.wait_ge(g_rdy, n + 1)
                s_.activation(sig_b, gate_b, ACT.Sigmoid, scale=1.702).then_inc(sig_rdy, 1)

            def y_evac(n, s, stored):
                act.wait_ge(dn_used, KT * (n + 1))
                if stored is not None:
                    act.wait_ge(y_out[s], 16 * stored)
                s_.activation(ysb[s].rearrange("p (b c) -> p b c", b=2), ps[:, 6:8, :], ACT.Copy).then_inc(y_ev, 1)
                act.wait_ge(y_ev, n + 1)
                act.dma_start(y_d[bass.ds(n * BLK, BLK), :], ysb[s]).then_inc(y_out[s], 16)

            xt_evac(0, 0, None)
            sigmoid(0)
            xt_evac(1, 1, None)
            at_evac(0, True)
            sigmoid(1)
            for n in (2, 3):
                xt_evac(n, n % 2, 1)
                y_evac(n - 2, n % 2, None)
                at_evac(n - 1, False)
                sigmoid(n)
            with act.Fori(2, E // 2) as m:
                for s in range(2):
                    xt_evac(2 * m + s, s, 1)
                    y_evac(2 * m + s - 2, s, m - 1)
                    at_evac(2 * m + s - 1, False)
                    sigmoid(2 * m + s)
            y_evac(E - 2, 0, E // 2 - 1)
            at_evac(E - 1, False)
            y_evac(E - 1, 1, E // 2 - 1)
            ov = overflow_count(act)
            with act.If(ov > 0):
                with act.Fori(0, ov) as j:
                    xt_evac(E + j, 0, 0)
                    sigmoid(E + j)
                    at_evac(E + j, False)
                    y_evac(E + j, 0, E // 2 + j)
            for t in range(TT):
                act.wait_ge(x3_rdy, t + 1)
                s_.activation(yg[t % 2][0], comb[t % 2], ACT.Square, accum_out=ss[:, t:t + 1]).then_inc(sq3_done, 1)
                act.wait_ge(ms3_rdy, t + 1)
                s_.activation(rstd[:, t:t + 1], rstd[:, t:t + 1], ACT.Sqrt).then_inc(rms3_rdy, 1)
                act.wait_ge(res_rdy, t + 1)
                act.dma_start(out[0, P * t:P * t + P, :], comb[t % 2]).then_inc(out_done[t % 2], 16)

        @block.vector
        def _(dve):
            n_chain = [0]

            def link(ins):
                n_chain[0] += 1
                ins.then_inc(dve_chain2, 1)
                dve.wait_ge(dve_chain2, n_chain[0])

            v = nc.vector

            def two(buf):
                return buf.rearrange("p (b c) -> p b c", b=2)

            dve.wait_ge(small2_in, 16 * 5)
            for part in range(3):
                for c in range(3):
                    cs_ = slice(1024 * c, 1024 * c + 1024)
                    link(v.tensor_copy(btmp, braw[:, cs_]))
                    v.tensor_copy(bparts[E * part:E * part + E, cs_], btmp)
                    link(v.tensor_tensor(braw[:, cs_], braw[:, cs_], btmp, ALU.subtract))
            link(v.scalar_tensor_tensor(out=mod[:, 4, :], in0=mod[:, 4, :], scalar=1.0, in1=norm2B,
                                        op0=ALU.add, op1=ALU.mult))

            def route(t):
                dve.wait_ge(lg_mm, t + 1)
                lg = lgs[:, t, :]
                link(v.tensor_tensor(lg, ps[:, 6 + t % 2, E * t:E * t + E], rb[:], ALU.add))
                link(v.max(top[:, t, :], lg))
                link(v.max_index(idxu[:, t, :], top[:, t, :], lg))
                link(v.tensor_copy(idxf[:, t, :], idxu[:, t, :]))
                for k in range(TOPK):
                    link(v.tensor_scalar(oh[:, t, k, :], iotaE[:], idxf[:, t, k:k + 1], None, ALU.is_equal))
                link(v.tensor_reduce(rank[:, E * t:E * t + E], oh[:, t, :, :].rearrange("p k e -> p e k"), AX_X, ALU.add))
                v.tensor_copy(maskb[:, t, :], rank[:, E * t:E * t + E]).then_inc(mask_rdy, 1)

            for t in range(TT):
                pair_ = ps[:, 2 * (t % 2):2 * (t % 2) + 2, :]
                dve.wait_ge(p_mm, t + 1)
                if t >= 2:
                    dve.wait_ge(h2t_mm, t - 1)
                    dve.wait_ge(h2_out[t % 2], 16 * (t // 2))
                if t == 0:
                    dve.wait_ge(x_in, 32)
                link(v.tensor_tensor(two(h2[t % 2]), pair_, two(mod[:, 2, :]), ALU.mult))
                v.tensor_tensor(x2[:, t, :], x2[:, t, :], h2[t % 2], ALU.add).then_inc(x2_rdy, 1)
                dve.wait_ge(sq2_done, t + 1)
                v.tensor_scalar(rstd[:, t:t + 1], ss[:, t:t + 1], 1.0 / D, NORM_EPS, ALU.mult, ALU.add).then_inc(ms2_rdy, 1)
                dve.wait_ge(rms2_rdy, t + 1)
                link(v.reciprocal(rstd[:, t:t + 1], rstd[:, t:t + 1]))
                link(v.scalar_tensor_tensor(out=h2[t % 2], in0=x2[:, t, :], scalar=rstd[:, t:t + 1], in1=mod[:, 4, :],
                                            op0=ALU.mult, op1=ALU.mult))
                v.tensor_tensor(h2[t % 2], h2[t % 2], mod[:, 3, :], ALU.add).then_inc(h2_rdy, 1)
                if t:
                    route(t - 1)
            route(TT - 1)
            dve.wait_ge(rank_mm, 1)
            link(v.tensor_copy(cnt[:], ps[:, 7, TT * E:TT * E + E]))
            link(v.tensor_copy(rank[:], ps[:, 7, 0:TT * E]))
            link(v.tensor_scalar(ovf[:], cnt[:], float(BLK + 1), None, ALU.is_ge))
            for b in range(2, S // BLK):
                link(v.scalar_tensor_tensor(out=ovf[:], in0=cnt[:], scalar=float(BLK * b + 1), in1=ovf[:],
                                            op0=ALU.is_ge, op1=ALU.add))
            link(v.tensor_tensor_scan(out=ovc[:], data0=ovf[:], data1=zeroE[:], initial=0.0, op0=ALU.add, op1=ALU.add))
            link(v.tensor_tensor(cnt[:], ovc[:], ovf[:], ALU.subtract))
            link(v.tensor_scalar(cnt[:], cnt[:], float(BLK), float((E - 1) * BLK), ALU.mult, ALU.add))
            link(v.tensor_scalar(ovf[:], iotaE[:], float(BLK), None, ALU.mult))
            link(v.tensor_tensor(cnt[:], cnt[:], ovf[:], ALU.subtract))
            r3 = rank[:].rearrange("p (t e) -> p t e", t=TT)
            g3 = rge[:].rearrange("p (t e) -> p t e", t=TT)
            over_t = lambda m: m.unsqueeze(1).to_broadcast([P, TT, E])
            link(v.tensor_scalar(rge[:], rank[:], float(BLK), None, ALU.is_ge))
            link(v.tensor_tensor(g3, g3, over_t(cnt[:]), ALU.mult))
            link(v.tensor_tensor(r3, r3, g3, ALU.add))
            link(v.tensor_tensor(r3, r3, over_t(ovf[:]), ALU.add))
            link(v.tensor_tensor(oh[:], oh[:], r3.unsqueeze(2).to_broadcast([P, TT, TOPK, E]), ALU.mult))
            link(v.tensor_reduce(slotf[:], oh[:].rearrange("p t k e -> p (t k) e"), AX_X, ALU.add))
            link(v.tensor_copy(slotI[:], slotf[:]))
            link(v.tensor_scalar(ti[:], slotI[:], 7, None, ALU.logical_shift_right))
            link(v.tensor_copy(tf[:], ti[:]))
            link(v.scalar_tensor_tensor(out=slotf[:], in0=tf[:], scalar=-float(BLK), in1=slotf[:],
                                        op0=ALU.mult, op1=ALU.add))
            link(v.scalar_tensor_tensor(out=slotf[:], in0=slotf[:], scalar=float(NB), in1=tf[:],
                                        op0=ALU.mult, op1=ALU.add))
            v.tensor_copy(tabI[:], slotf[:]).then_inc(slots_rdy, 1)
            cmp = oh[:].rearrange("p t k e -> p (t k) e")
            link(v.tensor_tensor(cmp[:, 0:MAXOV, :], ovc[:].unsqueeze(1).to_broadcast([P, MAXOV, E]),
                                 iotaJ[:].unsqueeze(2).to_broadcast([P, MAXOV, E]), ALU.is_le))
            link(v.tensor_reduce(ovx[:, 0:MAXOV], cmp[:, 0:MAXOV, :], AX_X, ALU.add))
            link(v.tensor_scalar(ovx[:, 0:MAXOV], ovx[:, 0:MAXOV], float(E - 1), None, ALU.min))
            link(v.tensor_copy(ovx[:, MAXOV:MAXOV + 1], ovc[:, E - 1:E]))
            v.tensor_copy(ovI[:], ovx[:]).then_inc(ov_rdy, 1)
            v.tensor_tensor(gates[:], top[:, :, 0:TOPK], top[:, :, 0:1].to_broadcast([P, TT, TOPK]),
                            ALU.subtract).then_inc(gdif_rdy, 1)
            dve.wait_ge(gexp_rdy, 1)
            link(v.tensor_reduce(gsum[:], gates[:], AX_X, ALU.add))
            link(v.reciprocal(gsum[:], gsum[:]))
            link(v.tensor_tensor(gates[:], gates[:], gsum[:].unsqueeze(2).to_broadcast([P, TT, TOPK]), ALU.mult))

            def swiglu(n):
                dve.wait_ge(gu_used, KT * (n + 1))
                v.tensor_scalar(two(gate_b), ps[:, 0:2, :], 7.0, None, ALU.min).then_inc(g_rdy, 1)
                v.tensor_scalar(two(up_b), ps[:, 2:4, :], -7.0, 7.0, ALU.max, ALU.min).then_inc(sw_rd, 1)
                dve.wait_ge(sig_rdy, n + 1)
                v.tensor_tensor(gate_b, gate_b, sig_b, ALU.mult).then_inc(gs_rdy, 1)
                dve.wait_ge(gs_rdy, n + 1)
                dve.wait_ge(sw_rd, n + 1)

            def act_out(n, first):
                if not first:
                    dve.wait_ge(at_mm, n)
                v.scalar_tensor_tensor(out=actv, in0=up_b, scalar=1.0, in1=gate_b, op0=ALU.add,
                                       op1=ALU.mult).then_inc(act_rdy, 1)
                dve.wait_ge(act_rdy, n + 1)

            swiglu(0)
            act_out(0, True)
            with dve.Fori(1, E) as n:
                swiglu(n)
                act_out(n, False)
            ov = overflow_count(dve)
            with dve.If(ov > 0):
                with dve.Fori(0, ov) as j:
                    swiglu(E + j)
                    act_out(E + j, False)
            dve.wait_ge(normf_in, 16)
            for t in range(TT):
                y = yg[t % 2]
                c = comb[t % 2]
                dve.wait_ge(yg_in[t % 2], 16 * TOPK * (t // 2 + 1))
                if t >= 2:
                    dve.wait_ge(out_done[t % 2], 16)
                link(v.tensor_scalar(c, y[0], gates[:, t, 0:1], None, ALU.mult))
                for k in range(1, TOPK):
                    link(v.scalar_tensor_tensor(out=c, in0=y[k], scalar=gates[:, t, k:k + 1], in1=c,
                                                op0=ALU.mult, op1=ALU.add))
                link(v.tensor_tensor(c, c, mod[:, 5, :], ALU.mult))
                v.tensor_tensor(c, c, x2[:, t, :], ALU.add).then_inc(x3_rdy, 1)
                dve.wait_ge(sq3_done, t + 1)
                v.tensor_scalar(rstd[:, t:t + 1], ss[:, t:t + 1], 1.0 / D, NORM_EPS, ALU.mult, ALU.add).then_inc(ms3_rdy, 1)
                dve.wait_ge(rms3_rdy, t + 1)
                v.reciprocal(rstd[:, t:t + 1], rstd[:, t:t + 1]).then_inc(comb_done, 1)
                dve.wait_ge(comb_done, t + 1)
                v.scalar_tensor_tensor(out=c, in0=c, scalar=rstd[:, t:t + 1], in1=normfB, op0=ALU.mult,
                                       op1=ALU.mult).then_inc(res_rdy, 1)

        @block.tensor
        def _(pe):
            mm = nc.tensor.matmul

            def project(t):
                pe.wait_ge(wout_in, 16)
                if t == 0:
                    read_by(pe, ("pm", CT - 1))
                    pe.wait_ge(rw_out, 2)
                if t >= 2:
                    pe.wait_ge(x2_rdy, t - 1)
                for n, m in enumerate((2, 3, 4, 5, 6, 7, 0, 1)):
                    for c in range(2):
                        ins = mm(ps[:, 2 * (t % 2) + c, :], mixed[m][:, P * t:P * t + P],
                                 w_out_sb[:, m, 512 * c:512 * c + 512], start=(n == 0), stop=(n == KT - 1))
                ins.then_inc(p_mm, 1)

            def turn(t):
                pe.wait_ge(h2_rdy, t + 1)
                if t:
                    pe.wait_ge(h2t_ev, t)
                for k in range(KT):
                    ins = nc.tensor.transpose(ps[:, 4 + k // 4, P * (k % 4):P * (k % 4) + P],
                                              h2[t % 2][:, P * k:P * k + P], ident[:])
                ins.then_inc(h2t_mm, 1)

            def router(t):
                pe.wait_ge(h2t_ev, t + 1)
                pe.wait_ge(small2_in, 16 * 5)
                for k in range(KT):
                    ins = mm(ps[:, 6 + t % 2, E * t:E * t + E], h2T[:, k, :], rw_sb[:, k, :], start=(k == 0), stop=(k == KT - 1))
                ins.then_inc(lg_mm, 1)

            project(0)
            project(1)
            for t in range(TT):
                turn(t)
                router(t)
                if t + 2 < TT:
                    project(t + 2)
            pe.wait_ge(mask_rdy, TT)
            for t in range(TT + 1):
                o = ps[:, 7, E * t:E * t + E]
                for j in range(min(t + 1, TT)):
                    lhs = strictb if j == t else onesb
                    ins = mm(o, lhs[:], maskb[:, j, :], start=(j == 0), stop=(j == min(t, TT - 1)))
            ins.then_inc(rank_mm, 1)

            def xt(n, s, cnt):
                pe.wait_ge(xg_in[s], 16 * cnt)
                for k in range(KT):
                    ins = nc.tensor.transpose(ps[:, 4 + k // 4, P * (k % 4):P * (k % 4) + P],
                                              xg[s][:, P * k:P * k + P], ident[:])
                ins.then_inc(xt_mm, 1)

            def gate_up(n, s, e):
                pe.wait_ge(xt_ev, n + 1)
                for c in range(4):
                    mm(ps[:, c, :], bsel[:, bass.ds(e, 1)].to_broadcast([3 * E, P]),
                       bparts[0:3 * E, 512 * c:512 * c + 512], start=True, stop=False)
                for k in range(KT):
                    pe.wait_ge(gu_in[k], 16 * (n + 1))
                    for c in range(4):
                        ins = mm(ps[:, c, :], xT[s][:, k, :], w_gu_sb[:, k, 512 * c:512 * c + 512],
                                 start=False, stop=(k == KT - 1))
                    ins.then_inc(gu_used, 1)

            def at(n, xt_before):
                pe.wait_ge(act_rdy, n + 1)
                pe.wait_ge(xt_ev, xt_before)
                for k in range(KT):
                    ins = nc.tensor.transpose(ps[:, 4 + k // 4, P * (k % 4):P * (k % 4) + P],
                                              actv[:, P * k:P * k + P], ident[:])
                ins.then_inc(at_mm, 1)

            def down(n, e):
                pe.wait_ge(at_ev, n + 1)
                for c in range(2):
                    mm(ps[:, 6 + c, :], bsel[:, bass.ds(e, 1)].to_broadcast([3 * E, P]),
                       bparts[0:3 * E, 2 * F + 512 * c:2 * F + 512 * c + 512], start=True, stop=False)
                for k in range(KT):
                    pe.wait_ge(dn_in[k], 16 * (n + 1))
                    for c in range(2):
                        ins = mm(ps[:, 6 + c, :], aTr[:, k, :], w_dn_sb[:, k, 512 * c:512 * c + 512],
                                 start=False, stop=(k == KT - 1))
                    ins.then_inc(dn_used, 1)

            def step(n, s, cnt, yn):
                pe.wait_ge(at_ev, n - 1)
                xt(n, s, cnt)
                if yn is not None:
                    pe.wait_ge(y_ev, yn)
                down(n - 2, n - 2)
                at(n - 1, n + 1)
                pe.wait_ge(sw_rd, n)
                gate_up(n, s, n)

            pe.wait_ge(ov_rdy, 1)
            xt(0, 0, 1)
            gate_up(0, 0, 0)
            xt(1, 1, 1)
            at(0, 2)
            pe.wait_ge(sw_rd, 1)
            gate_up(1, 1, 1)
            step(2, 0, 2, None)
            step(3, 1, 2, 1)
            with pe.Fori(2, E // 2) as m:
                for s in range(2):
                    step(2 * m + s, s, m + 1, 2 * m + s - 2)
            pe.wait_ge(y_ev, E - 2)
            down(E - 2, E - 2)
            at(E - 1, E)
            pe.wait_ge(y_ev, E - 1)
            down(E - 1, E - 1)
            ov = overflow_count(pe)
            with pe.If(ov > 0):
                with pe.Fori(0, ov) as j:
                    n = E + j
                    e = pe.value_load(ovI[0:1, bass.ds(j, 1)], min_val=0, max_val=E - 1)
                    pe.wait_ge(at_ev, n)
                    xt(n, 0, E // 2 + 1 + j)
                    pe.wait_ge(sw_rd, n)
                    gate_up(n, 0, e)
                    at(n, n + 1)
                    pe.wait_ge(y_ev, n)
                    down(n, e)


_INS = ["x", "c", "ada_w", "ada_b", "norm1", "w_in", "w_out", "rwkv_mu", "rwkv_w0", "rwkv_w_up", "rwkv_a0",
        "rwkv_a_up", "rwkv_g_up", "rwkv_k_k", "rwkv_k_a", "rwkv_r_k", "rwkv_ln_w", "rwkv_ln_b", "pool_w",
        "pool_scale", "fox_b_f", "norm2", "router_w", "router_b", "moe_w_gu", "moe_b_gu", "moe_w_down",
        "moe_b_down", "norm_f"]


def kernel(**inputs):
    import concourse.bacc as _bacc
    from concourse.bass_utils import run_bass_kernel_spmd as _run

    nc = _bacc.Bacc("TRN2", target_bir_lowering=False, num_devices=1)
    arrays, args = {}, {}
    for name in _INS:
        arr = np.ascontiguousarray(inputs[name])
        arrays[f"in_{name}"] = arr
        args[name] = nc.dram_tensor(f"in_{name}", arr.shape, mybir.dt.from_np(arr.dtype), kind="ExternalInput").ap()
    out = nc.dram_tensor("out", (1, S, D), F32, kind="ExternalOutput").ap()
    build(nc, args, out)
    r = _run(nc, [arrays], core_ids=[0])
    return r.results[0]["out"]
```

```python
from contextlib import ExitStack

import numpy as np
import concourse.bass as bass
from concourse import mybir

F32 = mybir.dt.float32
F32R = mybir.dt.float32r
BF16 = mybir.dt.bfloat16
I32 = mybir.dt.int32
U32 = mybir.dt.uint32
ALU = mybir.AluOpType
ACT = mybir.ActivationFunctionType
AX_X = mybir.AxisListType.X

P = 128
D = 1024
S = 512
KT = D // P
TT = S // P
HD = 64
RW = 256
RH = RW // HD
CT = RW // P
CHUNK = 64
NC = S // CHUNK
POOL_WINDOWS = (2, 4, 8, 16)
PAD = max(POOL_WINDOWS)
FOX = 512
FH = FOX // HD
RWKV_IN = 1024
COL_POOL = RWKV_IN
COL_Q = COL_POOL + 256
COL_K = COL_Q + FOX
COL_V = COL_K + FOX
COL_F = COL_V + FOX
E = 32
TOPK = 4
F = 1024
BLK = 128
MAXOV = 15
NB = E + MAXOV
NORM_EPS = 1e-6
GN_EPS = 64e-5
DECAY = -float(np.exp(-0.5))
SM = HD ** -0.5
ADA_BLOCKS = 6 * D // 512
ADA_FIRST = 2 * D // 512
LEVELS = 6
SLOTS = 4
CHW = 2 * F
LATE = 5 * D

READERS = {"ada": "D", "hT": "A", "rw": "A", "q": "A", "lora": "A", "k": "A", "kkn": "A", "rk": "D",
           "v": "A", "pz": "A", "f": "AD", "pm": "A", "trAV": "A", "trBK": "D",
           "MP": "AD", "NP": "D", "M": "D", "T": "A", "XA": "D", "XB": "D", "NV": "A", "W": "A",
           "QY": "AD", "GH": "A"}
JOB_BANKS = 3


def plan():
    steps = [("ada", b) for b in range(4)]
    steps += [("hT", t, half) for t in range(TT) for half in range(2)]
    steps += [("rw", n) for n in range(8)]
    steps += [("q", n) for n in range(4)]
    steps += [("lora", n) for n in range(6)]
    steps += [("k", n) for n in range(4)]
    steps += [("kkn", ct) for ct in range(CT)] + [("rk", ct) for ct in range(CT)]
    steps += [("v", t) for t in range(TT)]
    steps += [("pz", 0), ("pz", 1), ("f", 0)]
    units = FH * TT
    early = 4
    steps += [("fox", u) for u in range(early)]
    steps += [("trAV", t) for t in range(TT)] + [("pm", 0)] + [("trBK", t) for t in range(TT)] + [("pm", 1)]
    solve = []
    for q in range(2):
        for j in range(2):
            t = 2 * q + j
            solve += [(kind, t, par) for kind in ("MP", "M", "NP") for par in range(2)]
        for lv in range(1, LEVELS):
            solve += [("T", 2 * q + j, lv) for j in range(2)]
            for j in range(2):
                if lv < LEVELS - 1:
                    solve.append(("XA", 2 * q + j, lv))
                solve.append(("XB", 2 * q + j, lv))
        for kind in ("NV", "W", "QY"):
            solve += [(kind, 2 * q + j) for j in range(2)]
        solve += [("GH", 2 * q + j, cc) for j in range(2) for cc in range(2)]
    late = []
    for b in range(ADA_FIRST, ADA_BLOCKS):
        late += [[("acc", b, 0)] + ([("ada", b - 1)] if b > ADA_FIRST else []), [("acc", b, 1)]]
    late.append([("ada", ADA_BLOCKS - 1)])
    done = early
    placed = 0
    for n, s in enumerate(solve):
        steps.append(s)
        if placed < len(late) and (n + 1) * (len(late) + 1) >= (placed + 1) * len(solve):
            steps += late[placed]
            placed += 1
        while (done - early) * len(solve) < (n + 1) * (units + 3 - early):
            steps.append(("fox", done))
            done += 1
    while done < units + 3:
        steps.append(("fox", done))
        done += 1
    return steps


STEPS = plan()
JOBS = [s for s in STEPS if s[0] not in ("fox", "acc")]
JOB = {s: n for n, s in enumerate(JOBS)}


def reads_through(engine, job):
    return sum(engine in READERS[s[0]] for s in JOBS[:JOB[job] + 1])


def build(nc, a, out):
    with ExitStack() as ctx:
        def sb(name, shape, dt=F32):
            return ctx.enter_context(nc.sbuf_tensor(name, shape, dt))

        def sem(name):
            return ctx.enter_context(nc.semaphore(name))

        R1 = sb("R1", [P, 25248 - LATE])

        def Rc(lo, hi):
            return R0[:, lo:hi] if hi <= LATE else R1[:, lo - LATE:hi - LATE]
        ident = sb("ident", [P, P])
        identb = sb("identb", [P, P], BF16)
        blockones = sb("blockones", [P, P])
        causal = sb("causal", [P, P], BF16)
        lvl = sb("lvl", [P, LEVELS, P])
        strict = sb("strict", [P, P])
        incl = sb("incl", [P, P])
        lvl0T = sb("lvl0T", [P, P])
        negsel = sb("negsel", [8, 8])
        scanmask = sb("scanmask", [P, S], BF16)
        cols = sb("cols", [P, 25])
        up = sb("up", [P, RW])
        g_up = sb("g_up", [P, RW])
        pool_w = sb("pool_w", [P, CT, HD])
        cT = sb("cT", [P, KT])
        cs = sb("cs", [P, KT])
        rcnt = sb("rcnt", [P, CT, PAD])
        fix = sb("fix", [P, PAD])
        ss = sb("ss", [P, TT])
        rstd = sb("rstd", [P, TT])
        gam = sb("gam", [P, CT, NC])
        fmx = sb("fmx", [P, 8])
        stmp = sb("stmp", [P, CT, HD])
        strictb = sb("strictb", [P, P], BF16)
        onesb = sb("onesb", [P, P], BF16)
        bsel = sb("bsel", [3 * E, E], BF16)
        iotaE = sb("iotaE", [P, E])
        iotaJ = sb("iotaJ", [P, MAXOV])
        zeroE = sb("zeroE", [P, E])
        epsc = sb("epsc", [P, 1])
        slotI = sb("slotI", [P, TT * TOPK], U32)
        ti = sb("ti", [P, TT * TOPK], U32)
        ovI = sb("ovI", [P, MAXOV + 1], I32)
        tok = sb("tok", [P, NB], U32)
        icol = [sb(f"icol{s}", [P, 1], U32) for s in range(2)]
        gates = sb("gates", [P, TT, TOPK])
        carried = sb("carried", [P, 2])

        early = ExitStack()
        R0 = early.enter_context(nc.sbuf_tensor("R0", [P, LATE], F32))
        Wt = early.enter_context(nc.sbuf_tensor("Wt", [P, 24576], F32))
        W3 = lambda off, x, y: Wt[:, off:off + x * y].rearrange("p (x y) -> p x y", x=x)
        R3 = lambda off, x, y: Rc(off, off + x * y).rearrange("p (x y) -> p x y", x=x)

        blk = [W3(4096 * s, KT, 512) for s in range(2)]
        def pair(off):
            return [W3(off + 512 * j, RH, P) for j in range(2)]
        MT, X, XT, Tm, ML, NT, PbT, PkT = [pair(1024 * n) for n in range(8)]
        W12 = [m.rearrange("p h (w k) -> p h w k", w=2) for m in ML]
        QT = W3(8192, CT, S)
        Yin = W3(9216, CT, S)
        GH = Wt[:, 10240:12288].rearrange("p (x c m) -> p x c m", x=CT, c=NC)
        tokA, tokV, tokB, tokK = [W3(12288 + 1024 * n, TT, RW) for n in range(4)]
        AR = Wt[:, 16384:18432].rearrange("p (x w t) -> p x w t", x=CT, w=2)
        Bt = W3(18432, CT, S)
        Kt = W3(19456, CT, S)
        Kh = W3(20480, CT, S)
        Bh = W3(21504, CT, S)
        L = W3(22528, CT, S)
        WG = W3(23552, 2, S)
        w_out_sb = W3(16384, KT, D)
        htmp = W3(16384, 2, D)
        norm1B = Wt[:, 18432:19456]
        lnY, lnC, lnS = [W3(1024 * n, CT, S) for n in range(3)]

        mod = [Rc(D * n, D * n + D) for n in range(6)]
        gT = R3(0, CT, S)
        rkv = R3(1024, CT, S)
        condB = R3(6144, KT, P)
        x_sb = R3(7168, TT, D)
        rT, kT, vT, aT = [R3(7168 + 1024 * n, CT, S) for n in range(4)]
        hT = R3(11264, KT, S)
        Pm = R3(11264, 3, S)
        PT = R3(12800, 2, S)
        tA = Rc(14304, 14832)
        tB = Rc(14832, 15360)
        fq = R3(15360, 4, S)
        fk = R3(17408, 4, S)
        fv = R3(19456, TT, FOX)
        cum = Rc(21504, 22016)
        fln = Rc(22016, 22528)
        pz = R3(22528, CT, S + PAD)
        pmix = R3(22528, CT, S)
        ST = Rc(23584, 24736).rearrange("p (x c v) -> p x c v", x=CT, c=9)
        fmin = Rc(24736, 25248)
        zraw = Rc(23584, 24612).rearrange("p (b t) -> p b t", b=2)

        MU, W0, A0, KK_, KA, RK, LNW, LNB, PSC = 0, 8, 10, 12, 14, 16, 18, 20, 22
        rw_sb = R3(6144, KT, E)
        rb = Rc(6400, 6432)
        lgs = R3(6432, TT, E)
        top = R3(6560, TT, 8)
        idxu = R3(6592, TT, 8).bitcast(U32)
        idxf = R3(6624, TT, 8)
        maskb = Rc(6656, 6720).bitcast(BF16).rearrange("p (t e) -> p t e", t=TT)
        rank = Rc(6720, 6848)
        rge = Rc(6848, 6976)
        cnt = Rc(6976, 7008)
        ovf = Rc(7008, 7040)
        ovc = Rc(7040, 7072)
        slotf = Rc(7072, 7088)
        tf = Rc(7088, 7104)
        ovx = Rc(7104, 7120)
        gsum = Rc(7120, 7124)
        oh = Rc(24736, 25248).rearrange("p (t k e) -> p t k e", t=TT, k=TOPK)
        lane_oh = R3(17408, TT * TOPK, BLK)
        block_oh = R3(19456, TT * TOPK, NB)
        iotaL = Rc(14336, 14336 + BLK)
        iotaB = Rc(14336 + BLK, 14336 + BLK + NB)
        tokf = Rc(14592, 14592 + TT)
        braw = Rc(17408, 20480)[0:E, :]
        norm2B = Rc(14336, 15360)
        xi = Wt[:, 0:P].bitcast(I32)
        yi = Wt[:, P:2 * P].bitcast(I32)

        h2_d = nc.dram_tensor("h2_rows", (S, D), F32, kind="Internal").ap()
        y_d = nc.dram_tensor("y_rows", (NB * BLK, D), F32, kind="Internal").ap()

        ps = ctx.enter_context(nc.psum_tensor("ps", [P, 8, 512], F32))
        job_bank = lambda job: ps[:, JOB[job] % JOB_BANKS, :]
        fox_s = lambda u: ps[:, 3 + u % 2, :]
        fox_t = lambda u: ps[:, 5 + u % 2, :]
        fox_o = ps[:, 7, :]

        x_in = sem("x_in")
        small_in = sem("small_in")
        bias_in = sem("bias_in")
        bias2_in = sem("bias2_in")
        ada_in = [sem(f"ada_in{h}") for h in range(2)]
        ada_acc = sem("ada_acc")
        blk_in = [sem(f"blk_in{s}") for s in range(2)]
        wout_in = sem("wout_in")
        cst_pool = sem("cst_pool")
        cst_dve = sem("cst_dve")
        cond_sig = sem("cond_sig")
        cond_rdy = sem("cond_rdy")
        sq_done = sem("sq_done")
        h_add = sem("h_add")
        ms_rdy = sem("ms_rdy")
        rms_rdy = sem("rms_rdy")
        var_rdy = sem("var_rdy")
        std_rdy = sem("std_rdy")
        job_mm = sem("job_mm")
        act_read = sem("act_read")
        dve_read = sem("dve_read")
        dve_chain = sem("dve_chain")
        act_chain = sem("act_chain")
        pool_chain = sem("pool_chain")
        shifted = sem("shifted")
        lora_in = sem("lora_in")
        kk_raw = sem("kk_raw")
        kk_sq = sem("kk_sq")
        rk_in = sem("rk_in")
        logs = sem("logs")
        exps = sem("exps")
        elem_dve = sem("elem_dve")
        kk_unit = sem("kk_unit")
        elem_pool = sem("elem_pool")
        pool_sum = sem("pool_sum")
        pooled = sem("pooled")
        f_ln = sem("f_ln")
        cum_rdy = sem("cum_rdy")
        solve_pool = sem("solve_pool")
        fox_sc = sem("fox_sc")
        fox_mx = sem("fox_mx")
        fox_ex = sem("fox_ex")
        fox_nm = sem("fox_nm")
        fox_tr = sem("fox_tr")
        fox_pa = sem("fox_pa")
        fox_pd = sem("fox_pd")
        fox_pv = sem("fox_pv")
        fox_oe = sem("fox_oe")
        st_zero = sem("st_zero")
        st_mm = sem("st_mm")
        st_new = sem("st_new")
        y_mm = sem("y_mm")
        y_sum = sem("y_sum")
        mean_mm = sem("mean_mm")
        y_cen = sem("y_cen")
        y_sq = sem("y_sq")
        var_mm = sem("var_mm")
        y_scl = sem("y_scl")
        y_aff = sem("y_aff")
        rw_out = sem("rw_out")
        small2_in = sem("small2_in")
        normf_in = sem("normf_in")
        p_mm = sem("p_mm")
        x2_rdy = sem("x2_rdy")
        sq2_done = sem("sq2_done")
        ms2_rdy = sem("ms2_rdy")
        rms2_rdy = sem("rms2_rdy")
        h2_rdy = sem("h2_rdy")
        h2t_mm = sem("h2t_mm")
        h2t_ev = sem("h2t_ev")
        lg_mm = sem("lg_mm")
        gdif_rdy = sem("gdif_rdy")
        gexp_rdy = sem("gexp_rdy")
        mask_rdy = sem("mask_rdy")
        rank_mm = sem("rank_mm")
        ov_rdy = sem("ov_rdy")
        iota_rdy = sem("iota_rdy")
        onehots = sem("onehots")
        tok_mm = sem("tok_mm")
        tok_rdy = sem("tok_rdy")
        y_zero = sem("y_zero")
        ic_rdy = sem("ic_rdy")
        xt_mm = sem("xt_mm")
        xt_ev = sem("xt_ev")
        sw_rd = sem("sw_rd")
        g_rdy = sem("g_rdy")
        sig_rdy = sem("sig_rdy")
        gs_rdy = sem("gs_rdy")
        act_rdy = sem("act_rdy")
        at_mm = sem("at_mm")
        at_ev = sem("at_ev")
        at_lo = sem("at_lo")
        xt_lo = sem("xt_lo")
        y_ev = sem("y_ev")
        x3_rdy = sem("x3_rdy")
        sq3_done = sem("sq3_done")
        rms3_rdy = sem("rms3_rdy")
        res_rdy = sem("res_rdy")
        dve_chain2 = sem("dve_chain2")
        h2_out = [sem(f"h2_out{s}") for s in range(2)]
        xg_in = [sem(f"xg_in{s}") for s in range(2)]
        y_out = [sem(f"y_out{s}") for s in range(2)]
        yg_in = [sem(f"yg_in{s}") for s in range(3)]
        out_done = [sem(f"out_done{s}") for s in range(2)]
        raw_in = [sem(f"raw_in{s}") for s in range(SLOTS)]
        hi_rdy = [sem(f"hi_rdy{s}") for s in range(SLOTS)]
        lo_rdy = [sem(f"lo_rdy{s}") for s in range(SLOTS)]
        w_used = [sem(f"w_used{s}") for s in range(SLOTS)]

        def par_heads(m, par):
            return m.rearrange("p (k q) t -> p k q t", q=2)[:, :, par, :]

        def job_done(eng, job):
            eng.wait_ge(job_mm, JOB[job] + 1)

        def read_by(eng, job):
            if "A" in READERS[job[0]]:
                eng.wait_ge(act_read, reads_through("A", job))
            if "D" in READERS[job[0]]:
                eng.wait_ge(dve_read, reads_through("D", job))

        ada_blk = lambda b: ("ada", b)
        BLOCKS = [ada_blk(b) for b in range(4)] + [("w_in", 0), ("w_in", 512), ("w_in", COL_Q),
                  ("w_in", COL_K), ("w_in", COL_V), ("pf", 0)]
        BLK_OF = {b: n for n, b in enumerate(BLOCKS)}
        LAST_JOB = [("ada", b) for b in range(4)] + [("rw", 3), ("rw", 7), ("q", 3), ("k", 3), ("v", 3),
                    ("f", 0)]
        ada_half = [W3(20480 + 2048 * h, KT // 2, 512) for h in range(2)]
        ones_row = condB[:, 0, :]

        block = ctx.enter_context(nc.Block())

        @block.sync
        def _(sp):
            sp.dma_start(x_sb, a["x"][0].rearrange("(t p) d -> p t d", p=P)).then_inc(x_in, 16)
            ada_v = a["ada_w"][0].rearrange("(p k) n -> p k n", p=P)
            win_v = a["w_in"][0].rearrange("(k p) n -> p k n", p=P)
            for n, (kind, c) in enumerate(BLOCKS):
                if n >= 2:
                    job_done(sp, LAST_JOB[n - 2])
                elif n == 0:
                    sp.wait_ge(cst_dve, 1)
                dst = blk[n % 2]
                if kind == "ada":
                    sp.dma_start(dst, ada_v[:, :, 512 * c:512 * c + 512]).then_inc(blk_in[n % 2], 16)
                elif kind == "w_in":
                    sp.dma_start(dst, win_v[:, :, c:c + 512]).then_inc(blk_in[n % 2], 16)
                else:
                    sp.dma_start(dst[:, :, 0:256], win_v[:, :, COL_POOL:COL_POOL + 256]).then_inc(blk_in[n % 2], 16)
                    sp.dma_start(dst[:, :, 256:256 + FH], win_v[:, :, COL_F:COL_F + FH]).then_inc(blk_in[n % 2], 16)
            sp.dma_start(Rc(2 * D, LATE), a["ada_b"][0, 2 * D:LATE].partition_broadcast(P)).then_inc(bias2_in, 16)
            sp.dma_start(Rc(LATE, 6 * D), a["ada_b"][0, LATE:6 * D].partition_broadcast(P)).then_inc(bias2_in, 16)
            job_done(sp, ("trBK", TT - 1))
            read_by(sp, ("trBK", TT - 1))
            for b in range(ADA_FIRST, ADA_BLOCKS):
                for h in range(2):
                    if b > ADA_FIRST:
                        if h == 0:
                            sp.wait_ge(ada_acc, 2 * (b - ADA_FIRST))
                        else:
                            job_done(sp, ("ada", b - 1))
                    sp.dma_start(ada_half[h], ada_v[:, KT // 2 * h:KT // 2 * (h + 1), 512 * b:512 * b + 512]
                                 ).then_inc(ada_in[h], 16)
            sp.dma_start(x_sb, a["x"][0].rearrange("(t p) d -> p t d", p=P)).then_inc(x_in, 16)
            read_by(sp, ("QY", TT - 1))
            job_done(sp, ("ada", ADA_BLOCKS - 1))
            sp.dma_start(w_out_sb, a["w_out"][0].rearrange("(k p) n -> p k n", p=P)).then_inc(wout_in, 16)
            sp.wait_ge(fox_oe, 4)
            sp.dma_start(rw_sb, a["router_w"][0].rearrange("(k p) e -> p k e", p=P)).then_inc(small2_in, 16)
            sp.dma_start(rb, a["router_b"][0].partition_broadcast(P)).then_inc(small2_in, 16)
            sp.dma_start(braw[:, 0:2 * F], a["moe_b_gu"][0]).then_inc(small2_in, 16)
            sp.dma_start(braw[:, 2 * F:3 * F], a["moe_b_down"][0]).then_inc(small2_in, 16)
            sp.dma_start(norm2B, a["norm2"][0].partition_broadcast(P)).then_inc(small2_in, 16)

        def blk_ready(eng, b):
            n = BLK_OF[b]
            count = 16 * (n // 2 + 1)
            pf = BLK_OF[("pf", 0)]
            if n % 2 == pf % 2 and n >= pf:
                count += 16
            eng.wait_ge(blk_in[n % 2], count)

        @block.gpsimd
        def _(pool):
            n_chain = [0]

            def link(ins):
                n_chain[0] += 1
                ins.then_inc(pool_chain, 1)
                pool.wait_ge(pool_chain, n_chain[0])

            g = nc.gpsimd
            link(g.memset(ident[:], 0.0))
            link(g.affine_select(out=ident[:], in_=ident[:], compare_op=ALU.not_equal, fill=1.0, base=0,
                                 pattern=[[-1, P]], channel_multiplier=1))
            link(g.memset(strict[:], 0.0))
            link(g.affine_select(out=strict[:], in_=strict[:], compare_op=ALU.is_ge, fill=1.0, base=0,
                                 pattern=[[-1, P]], channel_multiplier=1))
            link(g.tensor_copy(strictb[:], strict[:]))
            link(g.memset(onesb[:], 1.0))
            link(g.memset(zeroE[:], 0.0))
            link(g.memset(epsc[:], NORM_EPS))
            link(g.memset(bsel[:], 0.0))
            for part in range(3):
                link(g.affine_select(out=bsel[:], in_=bsel[:], compare_op=ALU.not_equal, fill=1.0, base=-E * part,
                                     pattern=[[-1, E]], channel_multiplier=1))
            link(g.iota(iotaE[:], pattern=[[1, E]], base=0, channel_multiplier=0,
                        allow_small_or_imprecise_dtypes=True))
            link(g.iota(iotaJ[:], pattern=[[1, MAXOV]], base=0, channel_multiplier=0,
                        allow_small_or_imprecise_dtypes=True))
            link(g.iota(xi, pattern=[[0, P]], base=0, channel_multiplier=1))
            link(g.iota(yi, pattern=[[1, P]], base=0, channel_multiplier=0))
            link(g.memset(blockones[:], 0.0))
            for h in range(2):
                link(g.memset(blockones[HD * h:HD * h + HD, HD * h:HD * h + HD], 1.0))
            link(g.memset(causal[:], 0.0))
            link(g.affine_select(out=causal[:], in_=causal[:], compare_op=ALU.is_ge, fill=-1e30, base=0,
                                 pattern=[[-1, P]], channel_multiplier=1))
            link(g.memset(negsel[:], 0.0))
            link(g.affine_select(out=negsel[:], in_=negsel[:], compare_op=ALU.not_equal, fill=-1.0 / SM, base=0,
                                 pattern=[[-1, 8]], channel_multiplier=1))
            link(g.tensor_copy(identb[:], ident[:]))
            link(g.memset(scanmask[:], 1.0))
            link(g.memset(scanmask[:].rearrange("p (c s) -> p c s", s=CHUNK)[:, :, 0:1], 0.0))
            link(g.iota(rcnt[:], pattern=[[0, CT], [1, PAD]], base=1, channel_multiplier=0,
                        allow_small_or_imprecise_dtypes=True))
            link(g.memset(pz[:, :, 0:PAD], 0.0))
            g.memset(zraw[:, :, 0:1], 0.0).then_inc(cst_pool, 1)

            job_done(pool, ("f", 0))
            zero_src = Wt[:, 10240:10240 + D]
            link(g.memset(zero_src, 0.0))
            pool.dma_start(y_d[E * BLK:NB * BLK, :].rearrange("(b p) d -> p b d", p=P),
                           zero_src.unsqueeze(1).to_broadcast([P, MAXOV, D])).then_inc(y_zero, 16)
            for ct in range(CT):
                read_by(pool, ("pz", ct))
                if ct:
                    job_done(pool, ("pm", 0))
                z = pz[:, ct, :]
                n = S + PAD
                link(g.tensor_tensor(tA[:, 1:n], z[:, 1:n], z[:, 0:n - 1], ALU.add))
                last = g.tensor_tensor(tB[:, 3:n], tA[:, 3:n], tA[:, 1:n - 2], ALU.add)
                if ct:
                    link(last)
                    link(g.tensor_tensor(tA[:, 7:n], tB[:, 7:n], tB[:, 3:n - 4], ALU.add))
                    last = g.tensor_tensor(tB[:, 15:n], tA[:, 15:n], tA[:, 7:n - 8], ALU.add)
                last.then_inc(pool_sum, 1)
                if ct == 0:
                    for c2 in range(CT):
                        pool.wait_ge(kk_unit, c2 + 1)
                        link(g.tensor_tensor(aT[:, c2, :], Bh[:, c2, :], aT[:, c2, :], ALU.mult))
                        pool.wait_ge(exps, c2 + 1)
                        link(g.tensor_tensor(Bt[:, c2, :], aT[:, c2, :], Kt[:, c2, :], ALU.mult))
                        pool.wait_ge(elem_dve, 2 * c2 + 1)
                        g.tensor_tensor(Bh[:, c2, :], aT[:, c2, :], Kh[:, c2, :], ALU.mult).then_inc(elem_pool, 1)

            pool.wait_ge(shifted, 8)
            g.memset(ST[:, :, 0, :], 0.0).then_inc(st_zero, 1)
            bc = lambda m: m.unsqueeze(1).to_broadcast([P, RH, P])
            for q in range(2):
                for j in range(2):
                    t = 2 * q + j
                    read_by(pool, ("MP", t, 1))
                    read_by(pool, ("M", t, 1))
                    g.tensor_tensor(X[j], X[j], bc(ident[:]), ALU.add).then_inc(solve_pool, 1)
                    g.tensor_tensor(XT[j], XT[j], bc(ident[:]), ALU.add).then_inc(solve_pool, 1)
                    g.tensor_tensor(ML[j], MT[j], bc(lvl[:, 1, :]), ALU.mult).then_inc(solve_pool, 1)
                for lv in range(2, LEVELS):
                    for j in range(2):
                        job_done(pool, ("T", 2 * q + j, lv - 1))
                        g.tensor_tensor(ML[j], MT[j], bc(lvl[:, lv, :]), ALU.mult).then_inc(solve_pool, 1)

        PER_PAIR = 6 + 2 * (LEVELS - 2)

        def ml_count(t, lv):
            q, j = t // 2, t % 2
            return PER_PAIR * q + (3 * (j + 1) if lv == 1 else 6 + 2 * (lv - 2) + j + 1)

        @block.scalar
        def _(act):
            n_chain = [0]

            def link(ins):
                n_chain[0] += 1
                ins.then_inc(act_chain, 1)
                act.wait_ge(act_chain, n_chain[0])

            s = nc.scalar
            with nc.allow_non_contiguous_dma(reason="per-channel parameters, one column each"):
                act.dma_start(cT[:], a["c"].rearrange("o (p k) -> p (o k)", p=P)).then_inc(small_in, 16)
                for name, col, w in (("rwkv_mu", MU, 8), ("rwkv_w0", W0, 2), ("rwkv_a0", A0, 2),
                                     ("rwkv_k_k", KK_, 2), ("rwkv_k_a", KA, 2), ("rwkv_ln_w", LNW, 2),
                                     ("rwkv_ln_b", LNB, 2), ("pool_scale", PSC, 2)):
                    act.dma_start(cols[:, col:col + w], a[name].rearrange("o (c p) -> p (o c)", p=P)
                                  ).then_inc(small_in, 16)
                act.dma_start(cols[:, RK:RK + 2], a["rwkv_r_k"][0].rearrange("(c h) d -> (h d) c", c=CT)
                              ).then_inc(small_in, 16)
                act.dma_start(cols[0:FH, 24:25], a["fox_b_f"].rearrange("o f -> f o")).then_inc(small_in, 16)
            act.dma_start(up[0:HD, :], a["rwkv_w_up"][0]).then_inc(small_in, 16)
            act.dma_start(up[HD:P, :], a["rwkv_a_up"][0]).then_inc(small_in, 16)
            act.dma_start(g_up[:], a["rwkv_g_up"][0]).then_inc(small_in, 16)
            act.dma_start(pool_w[:], a["pool_w"][0].rearrange("(c h) i o -> (h i) c o", c=CT)).then_inc(small_in, 16)
            act.dma_start(norm1B, a["norm1"][0].partition_broadcast(P)).then_inc(bias_in, 16)
            act.dma_start(Rc(0, 2 * D), a["ada_b"][0, 0:2 * D].partition_broadcast(P)).then_inc(bias_in, 16)
            act.wait_ge(small_in, 16 * 15)
            s.activation(cs[:], cT[:], ACT.Sigmoid).then_inc(cond_sig, 1)
            act.wait_ge(x_in, 16)
            for t in range(TT):
                if t >= 2:
                    act.wait_ge(sq_done, t - 1)
                s.activation(htmp[:, t % 2, :], x_sb[:, t, :], ACT.Square,
                             accum_out=ss[:, t:t + 1]).then_inc(sq_done, 1)

            act.wait_ge(ms_rdy, 1)
            s.activation(rstd[:], rstd[:], ACT.Sqrt).then_inc(rms_rdy, 1)

            for step in STEPS:
                kind = step[0]
                if kind == "fox":
                    u = step[1]
                    if u < FH * TT:
                        n = P * (u % TT + 1)
                        act.wait_ge(fox_mx, u + 1)
                        if u >= 3:
                            act.wait_ge(fox_tr, u - 2)
                        s.activation(Pm[:, u % 3, 0:n], fox_s(u)[:, 0:n], ACT.Exp, scale=SM,
                                     bias=fmx[:, 4 * (u % 2) + 1:4 * (u % 2) + 2],
                                     accum_out=fmx[:, 4 * (u % 2) + 2:4 * (u % 2) + 3]).then_inc(fox_ex, 1)
                    v = u - 2
                    if 0 <= v < FH * TT and v % 2 == 0:
                        n = P * (v % TT + 1)
                        act.wait_ge(fox_tr, v + 1)
                        if v >= 2:
                            act.wait_ge(fox_pv, v - 1)
                        s.activation(PT[:, v % 2, 0:n], fox_t(v)[:, 0:n], ACT.Copy).then_inc(fox_pa, 1)
                    w = u - 3
                    if w >= 0 and w % (2 * TT) == 2 * TT - 1:
                        act.wait_ge(fox_pv, w + 1)
                        s.activation(fq[:, w // (2 * TT), :], fox_o, ACT.Copy).then_inc(fox_oe, 1)
                    continue
                if kind == "acc" or "A" not in READERS[kind]:
                    continue
                if kind == "lora" and step[1] == 0:
                    act.wait_ge(shifted, 7)
                    s.activation(WG[0:HD, 0, :], WG[0:HD, 0, :], ACT.Tanh).then_inc(lora_in, 1)
                    act.wait_ge(shifted, 8)
                    s.activation(WG[:, 1, :], WG[:, 1, :], ACT.Sigmoid).then_inc(lora_in, 1)
                if kind == "rw" and step[1] >= 2:
                    act.wait_ge(shifted, step[1] - 1)
                if kind == "kkn" and step[1] == 0:
                    for ct in range(CT):
                        act.wait_ge(kk_raw, ct + 1)
                        s.activation(Kh[:, ct, :], Bh[:, ct, :], ACT.Square).then_inc(kk_sq, 1)
                if kind == "pz" and step[1] == 0:
                    for ct in range(CT):
                        act.wait_ge(logs, ct + 1)
                        job_done(act, ("rk", ct))
                        s.activation(AR[:, ct, 1, :], L[:, ct, :], ACT.Exp)
                        s.activation(AR[:, ct, 0, :], AR[:, ct, 0, :], ACT.Exp)
                        s.activation(Kt[:, ct, :], L[:, ct, :], ACT.Exp, scale=-1.0)
                        s.activation(Kh[:, ct, :], Kh[:, ct, :], ACT.Exp)
                        s.activation(gam[:, ct, :], L[:, ct, :].rearrange("p (c s) -> p c s", s=CHUNK)[:, :, CHUNK - 1],
                                     ACT.Exp).then_inc(exps, 1)
                job_done(act, step)
                if "D" in READERS[kind]:
                    act.wait_ge(dve_read, reads_through("D", step))
                b = job_bank(step)
                if kind == "hT":
                    t, half = step[1], step[2]
                    ins = s.activation(hT[:, 4 * half:4 * half + 4, P * t:P * t + P],
                                       b.rearrange("p (k t) -> p k t", k=4), ACT.Copy)
                elif kind == "rw":
                    ins = s.activation(zraw[:, step[1] % 2, 1:S + 1], b, ACT.Copy)
                elif kind == "q":
                    ins = s.activation(fq[:, step[1], :], b, ACT.Copy)
                elif kind == "k":
                    ins = s.activation(fk[:, step[1], :], b, ACT.Copy)
                elif kind == "v":
                    ins = s.activation(fv[:, step[1], :], b, ACT.Copy)
                elif kind == "kkn":
                    act.wait_ge(rk_in, step[1] + 1)
                    ins = s.activation(AR[:, step[1], 0, :], b, ACT.Sqrt)
                elif kind == "lora":
                    what, ct = step[1] // 2, step[1] % 2
                    if what == 0:
                        ins = s.activation(Bt[:, ct, :], b, ACT.Sigmoid, bias=cols[:, W0 + ct:W0 + ct + 1])
                    elif what == 1:
                        ins = s.activation(aT[:, ct, :], b, ACT.Sigmoid, bias=cols[:, A0 + ct:A0 + ct + 1])
                    else:
                        ins = s.activation(gT[:, ct, :], b, ACT.Copy)
                elif kind == "pz":
                    ins = s.activation(pz[:, step[1], PAD:PAD + S], b, ACT.Copy)
                elif kind == "f":
                    ins = s.activation(fln[0:FH, :], b[0:FH, :], ACT.Abs, bias=cols[0:FH, 24:25])
                elif kind == "pm":
                    ct = step[1]
                    act.wait_ge(pooled, ct + 1)
                    ins = s.activation(pmix[:, ct, :], b, ACT.Copy, scale=cols[:, PSC + ct:PSC + ct + 1])
                elif kind == "trAV":
                    t = step[1]
                    ins = s.activation(Wt[:, 12288:14336].rearrange("p (w t c) -> p w t c", w=2, t=TT)[:, :, t, :],
                                       b.rearrange("p (w c) -> p w c", w=2), ACT.Copy)
                elif kind == "MP":
                    t, par = step[1], step[2]
                    if t >= 2:
                        act.wait_ge(solve_pool, PER_PAIR)
                    ins = s.activation(par_heads(MT[t % 2], par),
                                       b.rearrange("p (h w t) -> p h w t", h=2, w=2)[:, :, 0, :], ACT.Copy)
                elif kind == "T":
                    ins = s.activation(Tm[step[1] % 2], b.rearrange("p (h t) -> p h t", h=RH), ACT.Copy)
                elif kind == "NV":
                    ins = s.activation(Tm[step[1] % 2][:, :, 0:HD],
                                       b[:, 0:RW].rearrange("p (h v) -> p h v", h=RH), ACT.Copy)
                elif kind == "W":
                    ins = s.activation(ML[step[1] % 2], b.rearrange("p (h m) -> p h m", h=RH), ACT.Copy)
                elif kind == "QY":
                    t = step[1]
                    ins = s.activation(Yin[:, :, P * t:P * t + P],
                                       b.rearrange("p (c w t) -> p c w t", c=CT, w=2)[:, :, 1, :], ACT.Copy)
                elif kind == "GH":
                    t, cc = step[1], step[2]
                    act.wait_ge(y_zero, 16)
                    ins = s.activation(GH[:, :, 2 * t + cc, :], b[:, 0:RW].rearrange("p (x m) -> p x m", x=CT), ACT.Copy)
                ins.then_inc(act_read, 1)
                if kind == "f":
                    act.wait_ge(act_read, reads_through("A", step))
                    link(s.activation(fln[0:FH, :], fln[0:FH, :], ACT.Exp, scale=-1.0))
                    s.activation(fln[0:FH, :], fln[0:FH, :], ACT.Ln, bias=1.0).then_inc(f_ln, 1)

            for ct in range(CT):
                act.wait_ge(y_cen, ct + 1)
                s.activation(lnS[:, ct, :], lnC[:, ct, :], ACT.Square).then_inc(y_sq, 1)
            for ct in range(CT):
                act.wait_ge(var_rdy, ct + 1)
                s.activation(lnY[:, ct, :], lnY[:, ct, :], ACT.Sqrt).then_inc(std_rdy, 1)
            for ct in range(CT):
                act.wait_ge(y_scl, ct + 1)
                s.activation(lnC[:, ct, :], lnC[:, ct, :], ACT.Identity, scale=cols[:, LNW + ct:LNW + ct + 1],
                             bias=cols[:, LNB + ct:LNB + ct + 1]).then_inc(y_aff, 1)

        @block.vector
        def _(dve):
            n_chain = [0]

            def link(ins):
                n_chain[0] += 1
                ins.then_inc(dve_chain, 1)
                dve.wait_ge(dve_chain, n_chain[0])

            v = nc.vector
            dve.wait_ge(cst_pool, 1)
            link(v.tensor_tensor(xi, xi, yi, ALU.bitwise_xor))
            xf = Wt[:, 2 * P:3 * P]
            link(v.tensor_copy(xf, xi))
            ge = [Wt[:, (3 + n) * P:(4 + n) * P] for n in range(LEVELS + 1)]
            for n in range(LEVELS + 1):
                link(v.scalar_tensor_tensor(out=ge[n], in0=xf, scalar=float(1 << n), in1=strict[:],
                                            op0=ALU.is_ge, op1=ALU.mult))
            for n in range(LEVELS):
                link(v.tensor_tensor(lvl[:, n, :], ge[n], ge[n + 1], ALU.subtract))
            link(v.tensor_tensor(strict[:], strict[:], ge[LEVELS], ALU.subtract))
            link(v.tensor_tensor(incl[:], strict[:], ident[:], ALU.add))
            link(v.tensor_scalar(lvl0T[:], xf, 1.0, None, ALU.is_equal))
            link(v.tensor_tensor(lvl0T[:], lvl0T[:], lvl[:, 0, :], ALU.subtract))
            for ct in range(CT):
                for h in range(2):
                    w = float(POOL_WINDOWS[2 * ct + h])
                    link(v.tensor_scalar(rcnt[HD * h:HD * h + HD, ct, :], rcnt[HD * h:HD * h + HD, ct, :], w, None, ALU.min))
            link(v.reciprocal(rcnt[:], rcnt[:]))
            v.memset(stmp[:], 0.0).then_inc(cst_dve, 1)
            dve.wait_ge(cond_sig, 1)
            link(v.tensor_tensor(cs[:], cs[:], cT[:], ALU.mult))
            v.tensor_copy(condB, cs[:].unsqueeze(2).to_broadcast([P, KT, P])).then_inc(cond_rdy, 1)
            dve.wait_ge(sq_done, TT)
            v.tensor_scalar(rstd[:], ss[:], 1.0 / D, NORM_EPS, ALU.mult, ALU.add).then_inc(ms_rdy, 1)
            dve.wait_ge(rms_rdy, 1)
            link(v.reciprocal(rstd[:], rstd[:]))

            z_dest = [rT[:, 0, :], rT[:, 1, :], kT[:, 0, :], kT[:, 1, :], vT[:, 0, :], vT[:, 1, :],
                      WG[:, 0, :], WG[:, 1, :]]
            bc2 = lambda m: m.unsqueeze(1).to_broadcast([P, 2, P])
            for step in STEPS:
                kind = step[0]
                if kind == "fox":
                    u = step[1]
                    if u < FH * TT:
                        n = P * (u % TT + 1)
                        dve.wait_ge(fox_sc, u + 1)
                        m = fmx[:, 4 * (u % 2):4 * (u % 2) + 4]
                        link(v.reduce_max(m[:, 0:1], fox_s(u)[:, 0:n], AX_X))
                        v.tensor_scalar(m[:, 1:2], m[:, 0:1], -SM, None, ALU.mult).then_inc(fox_mx, 1)
                    w = u - 1
                    if 0 <= w < FH * TT:
                        n = P * (w % TT + 1)
                        m = fmx[:, 4 * (w % 2):4 * (w % 2) + 4]
                        dve.wait_ge(fox_ex, w + 1)
                        link(v.reciprocal(m[:, 3:4], m[:, 2:3]))
                        v.tensor_scalar(Pm[:, w % 3, 0:n], Pm[:, w % 3, 0:n], m[:, 3:4], None,
                                        ALU.mult).then_inc(fox_nm, 1)
                    w = u - 2
                    if 0 <= w < FH * TT:
                        n = P * (w % TT + 1)
                        if w % 2:
                            dve.wait_ge(fox_tr, w + 1)
                            if w >= 2:
                                dve.wait_ge(fox_pv, w - 1)
                            v.tensor_copy(PT[:, w % 2, 0:n], fox_t(w)[:, 0:n]).then_inc(fox_pd, 1)
                    continue
                if kind == "acc":
                    b, h = step[1], step[2]
                    if (b, h) == (ADA_FIRST, 0):
                        link(v.memset(ones_row, 1.0))
                    dve.wait_ge(ada_in[h], 16 * (b - ADA_FIRST + 1))
                    w = ada_half[h]
                    for k in range(KT // 2):
                        c = cs[:, KT // 2 * h + k:KT // 2 * h + k + 1]
                        if k == 0 and h == 0:
                            ins = v.tensor_scalar(w[:, 0, :], w[:, 0, :], c, None, ALU.mult)
                        else:
                            before = w[:, k - 1, :] if k else ada_half[0][:, KT // 2 - 1, :]
                            ins = v.scalar_tensor_tensor(out=w[:, k, :], in0=w[:, k, :], scalar=c, in1=before,
                                                         op0=ALU.mult, op1=ALU.add)
                        if k < KT // 2 - 1:
                            link(ins)
                    ins.then_inc(ada_acc, 1)
                    dve.wait_ge(ada_acc, 2 * (b - ADA_FIRST) + h + 1)
                    continue
                if kind == "hT" and step[2] == 0:
                    t = step[1]
                    if t == 0:
                        dve.wait_ge(dve_read, 4)
                        link(v.scalar_tensor_tensor(out=mod[1], in0=mod[1], scalar=1.0, in1=norm1B,
                                                    op0=ALU.add, op1=ALU.mult))
                    if t >= 2:
                        job_done(dve, ("hT", t - 2, 1))
                    h = htmp[:, t % 2, :]
                    link(v.scalar_tensor_tensor(out=h, in0=x_sb[:, t, :], scalar=rstd[:, t:t + 1],
                                                in1=mod[1], op0=ALU.mult, op1=ALU.mult))
                    v.tensor_tensor(h, h, mod[0], ALU.add).then_inc(h_add, 1)
                if kind == "rw":
                    n = step[1]
                    read_by(dve, step)
                    zr = zraw[:, n % 2, :]
                    d = z_dest[n]
                    link(v.tensor_tensor(d, zr[:, 0:S], zr[:, 1:S + 1], ALU.subtract))
                    v.scalar_tensor_tensor(out=d, in0=d, scalar=cols[:, MU + n:MU + n + 1], in1=zr[:, 1:S + 1],
                                           op0=ALU.mult, op1=ALU.add).then_inc(shifted, 1)
                if kind == "q" and step[1] == 0:
                    dve.wait_ge(shifted, 8)
                    for ct in range(CT):
                        v.tensor_scalar(Bh[:, ct, :], kT[:, ct, :], cols[:, KK_ + ct:KK_ + ct + 1], None,
                                        ALU.mult).then_inc(kk_raw, 1)
                if kind == "k" and step[1] == 0:
                    for ct in range(CT):
                        read_by(dve, ("lora", 2 + ct))
                        link(v.tensor_scalar(AR[:, ct, 0, :], aT[:, ct, :], 1.0, cols[:, KA + ct:KA + ct + 1],
                                             ALU.subtract, ALU.mult))
                        dve.wait_ge(kk_raw, ct + 1)
                        link(v.scalar_tensor_tensor(out=kT[:, ct, :], in0=AR[:, ct, 0, :], scalar=1.0,
                                                    in1=kT[:, ct, :], op0=ALU.add, op1=ALU.mult))
                        v.scalar_tensor_tensor(out=AR[:, ct, 1, :], in0=rT[:, ct, :],
                                               scalar=cols[:, RK + ct:RK + ct + 1], in1=kT[:, ct, :],
                                               op0=ALU.mult, op1=ALU.mult).then_inc(rk_in, 1)
                    for ct in range(CT):
                        link(v.tensor_scalar(Bt[:, ct, :], Bt[:, ct, :], DECAY, None, ALU.mult))
                        link(v.tensor_tensor_scan(out=L[:, ct, :], data0=scanmask[:], data1=Bt[:, ct, :], initial=0.0,
                                                  op0=ALU.mult, op1=ALU.add))
                if kind == "kkn":
                    ct = step[1]
                    read_by(dve, step)
                    link(v.tensor_scalar(AR[:, ct, 0, :], AR[:, ct, 0, :], 1e-12, None, ALU.max))
                    link(v.reciprocal(AR[:, ct, 0, :], AR[:, ct, 0, :]))
                    v.tensor_tensor(Bh[:, ct, :], Bh[:, ct, :], AR[:, ct, 0, :], ALU.mult).then_inc(kk_unit, 1)
                    dve.wait_ge(kk_unit, ct + 1)
                    link(v.tensor_tensor(AR[:, ct, 0, :], L[:, ct, :], Bt[:, ct, :], ALU.subtract))
                    Lc = L[:, ct, :].rearrange("p (c s) -> p c s", s=CHUNK)
                    v.tensor_tensor(Kh[:, ct, :].rearrange("p (c s) -> p c s", s=CHUNK),
                                    Lc[:, :, CHUNK - 1:CHUNK].to_broadcast([P, NC, CHUNK]), Lc,
                                    ALU.subtract).then_inc(logs, 1)
                if "D" not in READERS[kind]:
                    continue
                job_done(dve, step)
                b = job_bank(step)
                if kind == "ada":
                    n = step[1]
                    if n < ADA_FIRST:
                        dve.wait_ge(bias_in, 32)
                    else:
                        dve.wait_ge(bias2_in, 32)
                    m = Rc(512 * n, 512 * n + 512)
                    ins = v.tensor_tensor(m, b, m, ALU.add)
                elif kind == "rk":
                    ct = step[1]
                    ins = v.tensor_tensor(rkv[:, ct, :], b, vT[:, ct, :], ALU.mult)
                elif kind == "f":
                    ins = v.tensor_scalar(fmin[0:FH, :], b[0:FH, :], cols[0:FH, 24:25], 0.0, ALU.add, ALU.min)
                elif kind == "trBK":
                    t = step[1]
                    ins = v.tensor_copy(Wt[:, 14336:16384].rearrange("p (w t c) -> p w t c", w=2, t=TT)[:, :, t, :],
                                        b.rearrange("p (w c) -> p w c", w=2))
                elif kind == "MP":
                    t, par = step[1], step[2]
                    j = t % 2
                    bv = b.rearrange("p (h w t) -> p h w t", h=2, w=2)
                    v.tensor_tensor(par_heads(XT[j], par), bv[:, :, 0, :], bc2(lvl[:, 0, :]), ALU.mult)
                    ins = v.tensor_tensor(par_heads(PbT[j], par), bv[:, :, 1, :], bc2(incl[:]), ALU.mult)
                elif kind == "M":
                    ins = v.tensor_tensor(par_heads(X[step[1] % 2], step[2]),
                                          b[:, 0:RW].rearrange("p (h t) -> p h t", h=2), bc2(lvl0T[:]), ALU.mult)
                elif kind == "NP":
                    t, par = step[1], step[2]
                    j = t % 2
                    bv = b.rearrange("p (h w t) -> p h w t", h=2, w=2)
                    v.tensor_tensor(par_heads(NT[j], par), bv[:, :, 0, :], bc2(strict[:]), ALU.mult)
                    ins = v.tensor_tensor(par_heads(PkT[j], par), bv[:, :, 1, :], bc2(incl[:]), ALU.mult)
                elif kind == "XA":
                    j = step[1] % 2
                    ins = v.tensor_tensor(X[j], b.rearrange("p (h t) -> p h t", h=RH), X[j], ALU.add)
                elif kind == "XB":
                    j = step[1] % 2
                    ins = v.tensor_tensor(XT[j], b.rearrange("p (h t) -> p h t", h=RH), XT[j], ALU.add)
                elif kind == "QY":
                    t = step[1]
                    ts = slice(P * t, P * t + P)
                    ins = v.tensor_tensor(QT[:, :, ts], b.rearrange("p (c w t) -> p c w t", c=CT, w=2)[:, :, 0, :],
                                          AR[:, :, 1, ts], ALU.add)
                ins.then_inc(dve_read, 1)
                if kind == "f":
                    dve.wait_ge(f_ln, 1)
                    dve.wait_ge(dve_read, reads_through("D", step))
                    v.tensor_tensor_scan(out=cum[0:FH, :], data0=fmin[0:FH, :], data1=fln[0:FH, :], initial=0.0,
                                         op0=ALU.add, op1=ALU.subtract).then_inc(cum_rdy, 1)
                    for ct in range(CT):
                        dve.wait_ge(exps, ct + 1)
                        v.scalar_tensor_tensor(out=AR[:, ct, 0, :], in0=Bh[:, ct, :], scalar=-1.0,
                                               in1=AR[:, ct, 0, :], op0=ALU.mult, op1=ALU.mult).then_inc(elem_dve, 1)
                        v.tensor_tensor(AR[:, ct, 1, :], rT[:, ct, :], AR[:, ct, 1, :], ALU.mult)
                        dve.wait_ge(elem_pool, ct + 1)
                        v.tensor_tensor(Kt[:, ct, :], kT[:, ct, :], Kt[:, ct, :], ALU.mult)
                        v.tensor_tensor(Kh[:, ct, :], kT[:, ct, :], Kh[:, ct, :], ALU.mult).then_inc(elem_dve, 1)
                if step in (("f", 0), ("trBK", TT - 1)):
                    ct = ("f", "trBK").index(kind)
                    dve.wait_ge(pool_sum, ct + 1)
                    for h in range(2):
                        hs = slice(HD * h, HD * h + HD)
                        tt = (tA, tB)[h][hs, :]
                        link(v.tensor_tensor(fix[hs, :], tt[:, PAD:2 * PAD], rcnt[hs, ct, :], ALU.mult))
                        link(v.tensor_tensor(fix[hs, :], fix[hs, :], pz[hs, ct, PAD:2 * PAD], ALU.subtract))
                        link(v.scalar_tensor_tensor(out=tt[:, PAD:PAD + S], in0=tt[:, PAD:PAD + S],
                                                    scalar=1.0 / POOL_WINDOWS[2 * ct + h], in1=pz[hs, ct, PAD:PAD + S],
                                                    op0=ALU.mult, op1=ALU.subtract))
                        last = v.tensor_copy(tt[:, PAD:2 * PAD], fix[hs, :])
                        if h == 0:
                            link(last)
                    last.then_inc(pooled, 1)

            dve.wait_ge(st_zero, 1)
            read_by(dve, ("GH", TT - 1, 1))
            for c in range(NC - 1):
                if c:
                    dve.wait_ge(st_new, c)
                for ct in range(CT):
                    ins = v.scalar_tensor_tensor(out=stmp[:, ct, :], in0=ST[:, ct, c, :], scalar=gam[:, ct, c:c + 1],
                                                 in1=GH[:, ct, c, HD:P], op0=ALU.mult, op1=ALU.add)
                link(ins)
                dve.wait_ge(st_mm, c + 1)
                v.tensor_tensor(ST[:, :, c + 1, :], ps[:, 5, 0:P].rearrange("p (x v) -> p x v", x=CT), stmp[:],
                                ALU.add).then_inc(st_new, 1)
            for ct in range(CT):
                dve.wait_ge(y_mm, 1)
                v.tensor_tensor(lnY[:, ct, :], ps[:, 3 + ct, :], Yin[:, ct, :], ALU.add).then_inc(y_sum, 1)
            for ct in range(CT):
                dve.wait_ge(mean_mm, ct + 1)
                v.scalar_tensor_tensor(out=lnC[:, ct, :], in0=ps[:, 6 + ct, :], scalar=-1.0 / HD, in1=lnY[:, ct, :],
                                       op0=ALU.mult, op1=ALU.add).then_inc(y_cen, 1)
            for ct in range(CT):
                dve.wait_ge(var_mm, ct + 1)
                v.tensor_scalar(lnY[:, ct, :], ps[:, 3 + ct, :], 1.0 / HD, GN_EPS, ALU.mult, ALU.add).then_inc(var_rdy, 1)
                dve.wait_ge(std_rdy, ct + 1)
                link(v.reciprocal(lnY[:, ct, :], lnY[:, ct, :]))
                v.tensor_tensor(lnC[:, ct, :], lnC[:, ct, :], lnY[:, ct, :], ALU.mult).then_inc(y_scl, 1)
            for ct in range(CT):
                dve.wait_ge(y_aff, ct + 1)
                link(v.tensor_tensor(rkv[:, ct, :], lnC[:, ct, :], rkv[:, ct, :], ALU.add))
                v.tensor_tensor(rkv[:, ct, :], rkv[:, ct, :], gT[:, ct, :], ALU.mult).then_inc(rw_out, 1)

        @block.tensor
        def _(pe):
            mm = nc.tensor.matmul

            def head(h):
                return HD * (h % 2), h // 2

            pe.wait_ge(cond_rdy, 1)
            pe.wait_ge(cst_dve, 1)
            for step in STEPS:
                kind = step[0]
                if kind == "acc":
                    continue
                if kind == "fox":
                    u = step[1]
                    if u < FH * TT:
                        h, i = u // TT, u % TT
                        po, ct = head(h)
                        n = P * (i + 1)
                        if u == 0:
                            pe.wait_ge(cum_rdy, 1)
                            read_by(pe, ("v", TT - 1))
                        if u >= 2:
                            pe.wait_ge(fox_ex, u - 1)
                        o = fox_s(u)[:, 0:n]
                        mm(o, fq[po:po + HD, ct, P * i:P * i + P], fk[po:po + HD, ct, 0:n], start=True, stop=False)
                        mm(o, negsel[:, h:h + 1].to_broadcast([8, P]), cum[0:FH, 0:n], start=False, stop=False)
                        mm(o[:, n - P:n], identb[:], causal[:], start=False, stop=True).then_inc(fox_sc, 1)
                    w = u - 2
                    if 0 <= w < FH * TT:
                        pe.wait_ge(fox_nm, w + 1)
                        if w >= 2:
                            pe.wait_ge(fox_pd if w % 2 else fox_pa, w // 2)
                        for kt in range(w % TT + 1):
                            ins = nc.tensor.transpose(fox_t(w)[:, P * kt:P * kt + P],
                                                      Pm[:, w % 3, P * kt:P * kt + P], ident[:])
                        ins.then_inc(fox_tr, 1)
                    w = u - 3
                    if 0 <= w < FH * TT:
                        h, i = w // TT, w % TT
                        po, ct = head(h)
                        pe.wait_ge(fox_pd if w % 2 else fox_pa, w // 2 + 1)
                        if ct and w % (2 * TT) == 0:
                            pe.wait_ge(fox_oe, ct)
                        for kt in range(i + 1):
                            ins = mm(fox_o[po:po + HD, P * i:P * i + P], fv[:, kt, HD * h:HD * h + HD],
                                     PT[:, w % 2, P * kt:P * kt + P], start=(kt == 0), stop=(kt == i))
                        ins.then_inc(fox_pv, 1)
                    continue
                n = JOB[step]
                if n >= JOB_BANKS:
                    read_by(pe, JOBS[n - JOB_BANKS])
                b = job_bank(step)
                if kind == "ada" and step[1] >= ADA_FIRST:
                    pe.wait_ge(ada_acc, 2 * (step[1] - ADA_FIRST + 1))
                    ins = mm(b, ones_row, ada_half[1][:, KT // 2 - 1, :], start=True, stop=True)
                elif kind == "ada":
                    c = step[1]
                    blk_ready(pe, ("ada", c))
                    w = blk[BLK_OF[("ada", c)] % 2]
                    for k in range(KT):
                        ins = mm(b, condB[:, k, :], w[:, k, :], start=(k == 0), stop=(k == KT - 1))
                elif kind == "hT":
                    t, half = step[1], step[2]
                    pe.wait_ge(h_add, t + 1)
                    for k in range(4):
                        ins = nc.tensor.transpose(b[:, P * k:P * k + P],
                                                  htmp[:, t % 2, P * (4 * half + k):P * (4 * half + k) + P], ident[:])
                elif kind in ("rw", "q", "k", "pz", "f"):
                    m = step[1]
                    if kind == "rw":
                        key, c = ("w_in", 512 * (m // 4)), P * (m % 4)
                        if m == 0:
                            read_by(pe, ("hT", TT - 1, 1))
                    elif kind in ("q", "k"):
                        key, c = ("w_in", COL_Q if kind == "q" else COL_K), P * m
                    else:
                        key, c = ("pf", 0), (P * m if kind == "pz" else 2 * P)
                    rows = FH if kind == "f" else P
                    blk_ready(pe, key)
                    w = blk[BLK_OF[key] % 2]
                    for k in range(KT):
                        ins = mm(b[0:rows, :], w[:, k, c:c + rows], hT[:, k, :], start=(k == 0), stop=(k == KT - 1))
                elif kind == "v":
                    t = step[1]
                    blk_ready(pe, ("w_in", COL_V))
                    w = blk[BLK_OF[("w_in", COL_V)] % 2]
                    for k in range(KT):
                        ins = mm(b, hT[:, k, P * t:P * t + P], w[:, k, :], start=(k == 0), stop=(k == KT - 1))
                elif kind == "lora":
                    what, ct = step[1] // 2, step[1] % 2
                    cs_ = slice(P * ct, P * ct + P)
                    pe.wait_ge(lora_in, 2)
                    if what == 0:
                        ins = mm(b, up[0:HD, cs_], WG[0:HD, 0, :], start=True, stop=True)
                    elif what == 1:
                        ins = mm(b, up[HD:P, cs_], WG[HD:P, 0, :], start=True, stop=True)
                    else:
                        ins = mm(b, g_up[:, cs_], WG[:, 1, :], start=True, stop=True)
                elif kind == "kkn":
                    pe.wait_ge(kk_sq, step[1] + 1)
                    ins = mm(b, blockones[:], Kh[:, step[1], :], start=True, stop=True)
                elif kind == "rk":
                    pe.wait_ge(rk_in, step[1] + 1)
                    ins = mm(b, blockones[:], AR[:, step[1], 1, :], start=True, stop=True)
                elif kind == "pm":
                    ct = step[1]
                    pe.wait_ge(pooled, ct + 1)
                    for h in range(2):
                        hs = slice(HD * h, HD * h + HD)
                        ins = mm(b[hs, :], pool_w[hs, ct, :], (tA, tB)[h][hs, PAD:PAD + S], start=True, stop=True)
                elif kind in ("trAV", "trBK"):
                    t = step[1]
                    ts = slice(P * t, P * t + P)
                    pe.wait_ge(elem_dve, 2 * CT)
                    pe.wait_ge(elem_pool, CT)
                    for w in range(2):
                        for ct in range(CT):
                            if kind == "trAV":
                                src = (AR[:, ct, 0, ts], vT[:, ct, ts])[w]
                            else:
                                src = (Bh[:, ct, ts], Kh[:, ct, ts])[w]
                            ins = nc.tensor.transpose(b[:, RW * w + P * ct:RW * w + P * ct + P], src, ident[:])
                else:
                    t = step[1]
                    j = t % 2
                    ts = slice(P * t, P * t + P)
                    if kind in ("MP", "NP"):
                        if t % 2 == 0 and kind == "MP" and step[2] == 0:
                            job_done(pe, ("f", 0))
                        for hh in range(2):
                            po, ct = head(2 * hh + step[2])
                            ins = mm(b[:, RW * hh:RW * hh + RW].rearrange("p (w t) -> p w t", w=2),
                                     (Bt if kind == "MP" else Kt)[po:po + HD, ct, ts], AR[po:po + HD, ct, :, ts],
                                     start=True, stop=True)
                    elif kind == "M":
                        for hh in range(2):
                            po, ct = head(2 * hh + step[2])
                            ins = mm(b[:, P * hh:P * hh + P], AR[po:po + HD, ct, 0, ts], Bt[po:po + HD, ct, ts],
                                     start=True, stop=True)
                    elif kind == "T":
                        lv = step[2]
                        pe.wait_ge(solve_pool, ml_count(t, lv))
                        if lv > 1:
                            read_by(pe, ("XA", t, lv - 1))
                        for h in range(RH):
                            ins = mm(b[:, P * h:P * h + P], ML[j][:, h, :], X[j][:, h, :], start=True, stop=True)
                    elif kind in ("XA", "XB"):
                        lv = step[2]
                        read_by(pe, ("T", t, lv))
                        if lv > 1:
                            read_by(pe, ("XB", t, lv - 1))
                        for h in range(RH):
                            lhs, rhs = (XT, Tm) if kind == "XA" else (Tm, XT)
                            ins = mm(b[:, P * h:P * h + P], lhs[j][:, h, :], rhs[j][:, h, :], start=True, stop=True)
                    elif kind == "NV":
                        read_by(pe, ("NP", t, 1))
                        for h in range(RH):
                            ins = mm(b[:, HD * h:HD * h + HD], NT[j][:, h, :], tokV[:, t, HD * h:HD * h + HD],
                                     start=True, stop=True)
                    elif kind == "W":
                        read_by(pe, ("NV", t))
                        read_by(pe, ("XB", t, LEVELS - 1))
                        for h in range(RH):
                            o = b[:, P * h:P * h + P]
                            mm(o[:, 0:HD], XT[j][:, h, :], tokA[:, t, HD * h:HD * h + HD], start=True, stop=True)
                            ins = mm(o[:, HD:P], XT[j][:, h, :], Tm[j][:, h, 0:HD], start=True, stop=True)
                    elif kind == "QY":
                        read_by(pe, ("W", t))
                        read_by(pe, ("NP", t, 1))
                        for h in range(RH):
                            po, ct = head(h)
                            o = b[po:po + HD, RW * ct:RW * ct + RW]
                            mm(o[:, 0:P], W12[j][:, h, 0, :], PbT[j][:, h, :], start=True, stop=True)
                            mm(o[:, P:2 * P], W12[j][:, h, 1, :], PbT[j][:, h, :], start=True, stop=False)
                            ins = mm(o[:, P:2 * P], tokV[:, t, HD * h:HD * h + HD], PkT[j][:, h, :],
                                     start=False, stop=True)
                    elif kind == "GH":
                        for h in range(RH):
                            po, ct = head(h)
                            hc = slice(HD * h, HD * h + HD)
                            rs = slice(CHUNK * step[2], CHUNK * step[2] + CHUNK)
                            o = b[po:po + HD, P * ct:P * ct + P]
                            mm(o[:, 0:HD], W12[j][rs, h, 0, :], tokB[rs, t, hc], start=True, stop=True)
                            mm(o[:, HD:P], tokB[rs, t, hc], W12[j][rs, h, 1, :], start=True, stop=False)
                            ins = mm(o[:, HD:P], tokK[rs, t, hc], tokV[rs, t, hc], start=False, stop=True)
                ins.then_inc(job_mm, 1)

            read_by(pe, ("GH", TT - 1, 1))
            read_by(pe, ("QY", TT - 1))
            pe.wait_ge(fox_oe, 4)
            pe.wait_ge(st_zero, 1)
            for c in range(NC):
                if c:
                    pe.wait_ge(st_new, c)
                if c < NC - 1:
                    for h in range(RH):
                        po, ct = head(h)
                        ins = mm(ps[po:po + HD, 5, HD * ct:HD * ct + HD], GH[po:po + HD, ct, c, 0:HD],
                                 ST[po:po + HD, ct, c, :], start=True, stop=True)
                    ins.then_inc(st_mm, 1)
                for h in range(RH):
                    po, ct = head(h)
                    ins = mm(ps[po:po + HD, 3 + ct, CHUNK * c:CHUNK * c + CHUNK], ST[po:po + HD, ct, c, :],
                             QT[po:po + HD, ct, CHUNK * c:CHUNK * c + CHUNK], start=True, stop=True)
            ins.then_inc(y_mm, 1)
            for ct in range(CT):
                pe.wait_ge(y_sum, ct + 1)
                mm(ps[:, 6 + ct, :], blockones[:], lnY[:, ct, :], start=True, stop=True).then_inc(mean_mm, 1)
            for ct in range(CT):
                pe.wait_ge(y_sq, ct + 1)
                mm(ps[:, 3 + ct, :], blockones[:], lnS[:, ct, :], start=True, stop=True).then_inc(var_mm, 1)
        x2 = x_sb
        h2 = [Rc(11264, 12288), Rc(12288, 13312)]
        h2T = Rc(13312, 14336).rearrange("p (k t) -> p k t", k=KT)
        early.close()
        xTh, xTl, aTh, aTl = [sb(name, [P, KT, BLK], F32R) for name in ("xTh", "xTl", "aTh", "aTl")]
        xg = [sb("xg0", [P, D])[:], Rc(17408, 18432)]
        w_raw = sb("w_raw", [P, SLOTS, CHW])
        w_hi = sb("w_hi", [P, SLOTS, CHW], F32R)
        w_lo = sb("w_lo", [P, SLOTS, CHW], F32R)
        actv = Rc(18432, 19456)
        gate_b, sig_b, up_b = Rc(11264, 12288), Rc(12288, 13312), Rc(13312, 14336)
        ysb = [Rc(15360, 16384), Rc(16384, 17408)]
        bparts = Rc(20480, 22016).bitcast(BF16)
        btmp = Rc(22016, 22528)[0:E, :].bitcast(BF16)
        normfB = Rc(23584, 24608)
        yg = [[w_raw[:, 2 * t + k // 2, D * (k % 2):D * (k % 2) + D] for k in range(TOPK)] for t in range(2)]
        yg.append([Rc(11264 + D * k, 12288 + D * k) for k in range(TOPK)])
        sq_junk = [Rc(17408, 18432), Rc(18432, 19456)]
        comb = ysb

        mixed = [rkv[:, 0, :], rkv[:, 1, :], pmix[:, 0, :], pmix[:, 1, :]] + [fq[:, m, :] for m in range(4)]


        def up_round(n):
            return 3 * n

        def down_round(n):
            return 3 * n + 5

        LAST_DOWN = 3 * E
        gu_v = a["moe_w_gu"][0].rearrange("e k n -> (e k) n")
        dn_v = a["moe_w_down"][0].rearrange("e k n -> (e k) n")

        def load_up(sp, e, k0, rnd):
            for s in range(SLOTS):
                if rnd is not None:
                    sp.wait_ge(lo_rdy[s], rnd - 1)
                sp.dma_start(w_raw[:, s, :], gu_v[bass.ds(e * D + P * (k0 + s), P), :]).then_inc(raw_in[s], 16)

        def load_down(sp, e, rnd):
            for s in range(SLOTS):
                sp.wait_ge(lo_rdy[s], rnd - 1)
                sp.dma_start(w_raw[:, s, :].rearrange("p (k n) -> p k n", k=2),
                             dn_v[bass.ds(e * F + 2 * P * s, 2 * P), :].rearrange("(k p) n -> p k n", k=2)
                             ).then_inc(raw_in[s], 16)

        def split_hi(eng, rnd, first=False):
            for s in range(SLOTS):
                if not first:
                    eng.wait_ge(w_used[s], rnd - 1)
                eng.wait_ge(raw_in[s], rnd * 16)
                nc.scalar.activation(w_hi[:, s, :], w_raw[:, s, :], ACT.Copy).then_inc(hi_rdy[s], 1)

        def split_lo(eng, engine, slots, rnd):
            for s in slots:
                eng.wait_ge(hi_rdy[s], rnd)
                engine.tensor_tensor(w_lo[:, s, :], w_raw[:, s, :], w_hi[:, s, :].bitcast(F32), ALU.subtract
                                     ).then_inc(lo_rdy[s], 1)

        DVE_SLOTS, POOL_SLOTS = range(SLOTS - 1), range(SLOTS - 1, SLOTS)

        def overflow_count(eng):
            eng.wait_ge(ov_rdy, 1)
            return eng.value_load(ovI[0:1, NB - E:NB - E + 1], min_val=0, max_val=MAXOV)

        @block.sync
        def _(sp):
            rw_free = rw_out
            sp.wait_ge(rw_free, 2)
            load_up(sp, 0, 0, None)
            sp.dma_start(normfB, a["norm_f"].partition_broadcast(P)).then_inc(normf_in, 16)
            load_up(sp, 0, SLOTS, 2)
            for half in range(2):
                load_up(sp, 1, SLOTS * half, 3 + half)
            with sp.Fori(2, E) as n:
                load_down(sp, n - 2, down_round(n - 2))
                for half in range(2):
                    load_up(sp, n, SLOTS * half, up_round(n) + half)
            load_down(sp, E - 2, down_round(E - 2))
            load_down(sp, E - 1, LAST_DOWN)
            ov = overflow_count(sp)
            with sp.If(ov > 0):
                with sp.Fori(0, ov) as j:
                    e = sp.value_load(ovI[0:1, bass.ds(j, 1)], min_val=0, max_val=E - 1)
                    for half in range(2):
                        load_up(sp, e, SLOTS * half, LAST_DOWN + 3 * j + (1 + half))
                    load_down(sp, e, LAST_DOWN + 3 * j + 3)

        @block.gpsimd
        def _(pool):
            def carry(c):
                nc.gpsimd.tensor_tensor(carried[:, c:c + 1], iotaE[:, 0:1], iotaE[:, 0:1], ALU.add)

            def gather(n, s, lag):
                if lag is not None:
                    pool.wait_ge(xt_mm, n - lag)
                    carry(0)
                nc.gpsimd.tensor_copy(icol[s][:], tok[:, bass.ds(n, 1)]).then_inc(ic_rdy, 1)
                pool.wait_ge(ic_rdy, n + 1)
                carry(1)
                nc.gpsimd.indirect_dma_start(out=xg[s], out_offset=None, in_=h2_d,
                                             in_offset=bass.IndirectOffsetOnAxis(ap=icol[s][:, 0:1], axis=0)
                                             ).then_inc(xg_in[s], 16)

            pool.wait_ge(h2_rdy, 1)
            lax = dict(allow_small_or_imprecise_dtypes=True)
            nc.gpsimd.iota(iotaL, pattern=[[1, BLK]], base=0, channel_multiplier=0, **lax)
            nc.gpsimd.iota(iotaB, pattern=[[1, NB]], base=0, channel_multiplier=0, **lax)
            nc.gpsimd.iota(tokf, pattern=[[P, TT]], base=0, channel_multiplier=1, **lax).then_inc(iota_rdy, 1)
            pool.wait_ge(tok_rdy, 1)
            for s in range(2):
                pool.wait_ge(h2_out[s], 16 * TT // 2)
            gather(0, 0, None)
            gather(1, 1, None)
            lo = lambda rnd: split_lo(pool, nc.gpsimd, POOL_SLOTS, rnd)
            for rnd in range(1, 4):
                lo(rnd)
            gather(2, 0, 1)
            for rnd in range(4, 6):
                lo(rnd)

            def step(n, s):
                if s is not None:
                    gather(n + 1, s, 1)
                lo(up_round(n))
                lo(up_round(n) + 1)
                lo(down_round(n - 1))

            with pool.Fori(1, E // 2 - 1) as m:
                for s in range(2):
                    step(2 * m + s, 1 - s)
            step(E - 2, 1)
            step(E - 1, None)
            lo(LAST_DOWN)
            ov = overflow_count(pool)
            with pool.If(ov > 0):
                with pool.Fori(0, ov) as j:
                    gather(E + j, 0, 0)
                    for r in range(3):
                        lo(LAST_DOWN + 3 * j + (1 + r))
            for s in range(SLOTS):
                pool.wait_ge(lo_rdy[s], LAST_DOWN + 3 * ov)
            pool.wait_ge(y_out[0], 16 * (E // 2) + 16 * ov)
            pool.wait_ge(y_out[1], 16 * (E // 2))
            carry(0)
            for t in range(TT):
                if t >= 3:
                    pool.wait_ge(x3_rdy, t - 2)
                for k in range(TOPK):
                    m = TOPK * t + k
                    nc.gpsimd.indirect_dma_start(out=yg[t % 3][k], out_offset=None, in_=y_d,
                                                 in_offset=bass.IndirectOffsetOnAxis(ap=slotI[:, m:m + 1], axis=0)
                                                 ).then_inc(yg_in[t % 3], 16)
            for s in range(2):
                pool.wait_ge(out_done[s], 32)

        @block.scalar
        def _(act):
            s_ = nc.scalar
            act.wait_ge(small2_in, 16 * 5)
            for t in range(TT):
                act.wait_ge(x2_rdy, t + 1)
                s_.activation(h2[t % 2], x2[:, t, :], ACT.Square, accum_out=ss[:, t:t + 1]).then_inc(sq2_done, 1)
                act.wait_ge(ms2_rdy, t + 1)
                s_.activation(rstd[:, t:t + 1], rstd[:, t:t + 1], ACT.Sqrt).then_inc(rms2_rdy, 1)
                act.wait_ge(h2_rdy, t + 1)
                act.dma_start(h2_d[P * t:P * t + P, :], h2[t % 2]).then_inc(h2_out[t % 2], 16)
                act.wait_ge(h2t_mm, t + 1)
                if t:
                    act.wait_ge(lg_mm, t)
                s_.activation(h2T, ps[:, 4:6, :].rearrange("p b (k t) -> p (b k) t", k=4), ACT.Copy).then_inc(h2t_ev, 1)
            act.wait_ge(gdif_rdy, 1)
            s_.activation(gates[:], gates[:], ACT.Exp).then_inc(gexp_rdy, 1)

            def turned(n, mm_sem, dst, ev_sem):
                act.wait_ge(mm_sem, n + 1)
                s_.activation(dst[:], ps[:, 4:6, :].rearrange("p b (k t) -> p (b k) t", k=4), ACT.Copy
                              ).then_inc(ev_sem, 1)

            def xt_evac(n):
                turned(n, xt_mm, xTh, xt_ev)

            def at_evac(n):
                turned(n, at_mm, aTh, at_ev)

            def sigmoid(n):
                act.wait_ge(g_rdy, n + 1)
                s_.activation(sig_b, gate_b, ACT.Sigmoid, scale=1.702).then_inc(sig_rdy, 1)

            def y_store(n, s):
                act.wait_ge(y_ev, n + 1)
                act.dma_start(y_d[bass.ds(n * BLK, BLK), :], ysb[s]).then_inc(y_out[s], 16)

            hi = lambda rnd: split_hi(act, rnd)
            split_hi(act, 1, first=True)
            xt_evac(0)
            hi(2)
            hi(3)
            sigmoid(0)
            xt_evac(1)
            at_evac(0)
            hi(4)
            hi(5)

            def step(n, s):
                sigmoid(n - 1)
                xt_evac(n)
                hi(up_round(n))
                y_store(n - 2, s)
                at_evac(n - 1)
                hi(up_round(n) + 1)
                hi(down_round(n - 1))

            with act.Fori(1, E // 2) as m:
                for s in range(2):
                    step(2 * m + s, s)
            sigmoid(E - 1)
            hi(LAST_DOWN)
            y_store(E - 2, 0)
            at_evac(E - 1)
            y_store(E - 1, 1)
            ov = overflow_count(act)
            with act.If(ov > 0):
                with act.Fori(0, ov) as j:
                    xt_evac(E + j)
                    hi(LAST_DOWN + 3 * j + 1)
                    hi(LAST_DOWN + 3 * j + 2)
                    sigmoid(E + j)
                    at_evac(E + j)
                    hi(LAST_DOWN + 3 * j + 3)
                    y_store(E + j, 0)
            for t in range(TT):
                act.wait_ge(x3_rdy, t + 1)
                s_.activation(sq_junk[t % 2], comb[t % 2], ACT.Square, accum_out=ss[:, t:t + 1]).then_inc(sq3_done, 1)
                act.wait_ge(sq3_done, t + 1)
                s_.activation(rstd[:, t:t + 1], ss[:, t:t + 1], ACT.Sqrt, scale=1.0 / D, bias=epsc[:]).then_inc(rms3_rdy, 1)
                if t:
                    act.wait_ge(res_rdy, t)
                    act.dma_start(out[0, P * (t - 1):P * t, :], comb[(t - 1) % 2]).then_inc(out_done[(t - 1) % 2], 16)
            act.wait_ge(res_rdy, TT)
            act.dma_start(out[0, P * (TT - 1):P * TT, :], comb[(TT - 1) % 2]).then_inc(out_done[(TT - 1) % 2], 16)

        @block.vector
        def _(dve):
            n_chain = [0]

            def link(ins):
                n_chain[0] += 1
                ins.then_inc(dve_chain2, 1)
                dve.wait_ge(dve_chain2, n_chain[0])

            v = nc.vector

            def two(buf):
                return buf.rearrange("p (b c) -> p b c", b=2)

            dve.wait_ge(small2_in, 16 * 5)
            for part in range(3):
                for c in range(3):
                    cs_ = slice(1024 * c, 1024 * c + 1024)
                    link(v.tensor_copy(btmp, braw[:, cs_]))
                    v.tensor_copy(bparts[E * part:E * part + E, cs_], btmp)
                    link(v.tensor_tensor(braw[:, cs_], braw[:, cs_], btmp, ALU.subtract))
            link(v.scalar_tensor_tensor(out=mod[4], in0=mod[4], scalar=1.0, in1=norm2B,
                                        op0=ALU.add, op1=ALU.mult))

            def route(t):
                dve.wait_ge(lg_mm, t + 1)
                lg = lgs[:, t, :]
                link(v.tensor_tensor(lg, ps[:, 6 + t % 2, E * t:E * t + E], rb[:], ALU.add))
                link(v.max(top[:, t, :], lg))
                link(v.max_index(idxu[:, t, :], top[:, t, :], lg))
                link(v.tensor_copy(idxf[:, t, :], idxu[:, t, :]))
                for k in range(TOPK):
                    link(v.tensor_scalar(oh[:, t, k, :], iotaE[:], idxf[:, t, k:k + 1], None, ALU.is_equal))
                link(v.tensor_reduce(rank[:, E * t:E * t + E], oh[:, t, :, :].rearrange("p k e -> p e k"), AX_X, ALU.add))
                v.tensor_copy(maskb[:, t, :], rank[:, E * t:E * t + E]).then_inc(mask_rdy, 1)

            for t in range(TT):
                pair_ = ps[:, 2 * (t % 2):2 * (t % 2) + 2, :]
                dve.wait_ge(p_mm, t + 1)
                if t >= 2:
                    dve.wait_ge(h2t_mm, t - 1)
                    dve.wait_ge(h2_out[t % 2], 16 * (t // 2))
                if t == 0:
                    dve.wait_ge(x_in, 32)
                link(v.tensor_tensor(two(h2[t % 2]), pair_, two(mod[2]), ALU.mult))
                v.tensor_tensor(x2[:, t, :], x2[:, t, :], h2[t % 2], ALU.add).then_inc(x2_rdy, 1)
                dve.wait_ge(sq2_done, t + 1)
                v.tensor_scalar(rstd[:, t:t + 1], ss[:, t:t + 1], 1.0 / D, NORM_EPS, ALU.mult, ALU.add).then_inc(ms2_rdy, 1)
                dve.wait_ge(rms2_rdy, t + 1)
                link(v.reciprocal(rstd[:, t:t + 1], rstd[:, t:t + 1]))
                link(v.scalar_tensor_tensor(out=h2[t % 2], in0=x2[:, t, :], scalar=rstd[:, t:t + 1], in1=mod[4],
                                            op0=ALU.mult, op1=ALU.mult))
                v.tensor_tensor(h2[t % 2], h2[t % 2], mod[3], ALU.add).then_inc(h2_rdy, 1)
                if t:
                    route(t - 1)
            route(TT - 1)
            dve.wait_ge(rank_mm, 1)
            link(v.tensor_copy(cnt[:], ps[:, 7, TT * E:TT * E + E]))
            link(v.tensor_copy(rank[:], ps[:, 7, 0:TT * E]))
            link(v.tensor_scalar(ovf[:], cnt[:], float(BLK + 1), None, ALU.is_ge))
            for b in range(2, S // BLK):
                link(v.scalar_tensor_tensor(out=ovf[:], in0=cnt[:], scalar=float(BLK * b + 1), in1=ovf[:],
                                            op0=ALU.is_ge, op1=ALU.add))
            link(v.tensor_tensor_scan(out=ovc[:], data0=ovf[:], data1=zeroE[:], initial=0.0, op0=ALU.add, op1=ALU.add))
            link(v.tensor_tensor(cnt[:], ovc[:], ovf[:], ALU.subtract))
            link(v.tensor_scalar(cnt[:], cnt[:], float(BLK), float((E - 1) * BLK), ALU.mult, ALU.add))
            link(v.tensor_scalar(ovf[:], iotaE[:], float(BLK), None, ALU.mult))
            link(v.tensor_tensor(cnt[:], cnt[:], ovf[:], ALU.subtract))
            r3 = rank[:].rearrange("p (t e) -> p t e", t=TT)
            g3 = rge[:].rearrange("p (t e) -> p t e", t=TT)
            over_t = lambda m: m.unsqueeze(1).to_broadcast([P, TT, E])
            link(v.tensor_scalar(rge[:], rank[:], float(BLK), None, ALU.is_ge))
            link(v.tensor_tensor(g3, g3, over_t(cnt[:]), ALU.mult))
            link(v.tensor_tensor(r3, r3, g3, ALU.add))
            link(v.tensor_tensor(r3, r3, over_t(ovf[:]), ALU.add))
            link(v.tensor_tensor(oh[:], oh[:], r3.unsqueeze(2).to_broadcast([P, TT, TOPK, E]), ALU.mult))
            link(v.tensor_reduce(slotf[:], oh[:].rearrange("p t k e -> p (t k) e"), AX_X, ALU.add))
            link(v.tensor_copy(slotI[:], slotf[:]))
            link(v.tensor_scalar(ti[:], slotI[:], 7, None, ALU.logical_shift_right))
            link(v.tensor_copy(tf[:], ti[:]))
            link(v.scalar_tensor_tensor(out=slotf[:], in0=tf[:], scalar=-float(BLK), in1=slotf[:],
                                        op0=ALU.mult, op1=ALU.add))
            dve.wait_ge(iota_rdy, 1)
            for m in range(TT * TOPK):
                t = m // TOPK
                v.tensor_scalar(lane_oh[:, m, :], iotaL, slotf[:, m:m + 1], None, ALU.is_equal)
                v.tensor_scalar(block_oh[:, m, :], iotaB, tf[:, m:m + 1], tokf[:, t:t + 1], ALU.is_equal,
                                ALU.mult).then_inc(onehots, 1)
            cmp = oh[:].rearrange("p t k e -> p (t k) e")
            link(v.tensor_tensor(cmp[:, 0:MAXOV, :], ovc[:].unsqueeze(1).to_broadcast([P, MAXOV, E]),
                                 iotaJ[:].unsqueeze(2).to_broadcast([P, MAXOV, E]), ALU.is_le))
            link(v.tensor_reduce(ovx[:, 0:MAXOV], cmp[:, 0:MAXOV, :], AX_X, ALU.add))
            link(v.tensor_scalar(ovx[:, 0:MAXOV], ovx[:, 0:MAXOV], float(E - 1), None, ALU.min))
            link(v.tensor_copy(ovx[:, MAXOV:MAXOV + 1], ovc[:, E - 1:E]))
            v.tensor_copy(ovI[:], ovx[:]).then_inc(ov_rdy, 1)
            dve.wait_ge(tok_mm, 1)
            v.tensor_copy(tok[:], ps[:, 6, 0:NB]).then_inc(tok_rdy, 1)
            v.tensor_tensor(gates[:], top[:, :, 0:TOPK], top[:, :, 0:1].to_broadcast([P, TT, TOPK]),
                            ALU.subtract).then_inc(gdif_rdy, 1)
            dve.wait_ge(gexp_rdy, 1)
            link(v.tensor_reduce(gsum[:], gates[:], AX_X, ALU.add))
            link(v.reciprocal(gsum[:], gsum[:]))
            link(v.tensor_tensor(gates[:], gates[:], gsum[:].unsqueeze(2).to_broadcast([P, TT, TOPK]), ALU.mult))

            def clamp(n, rnd):
                dve.wait_ge(w_used[SLOTS - 1], rnd)
                v.tensor_scalar(two(gate_b), ps[:, 0:2, :], 7.0, None, ALU.min).then_inc(g_rdy, 1)
                v.tensor_scalar(two(up_b), ps[:, 2:4, :], -7.0, 7.0, ALU.max, ALU.min).then_inc(sw_rd, 1)

            def swiglu(n, first=False):
                dve.wait_ge(sig_rdy, n + 1)
                v.tensor_tensor(gate_b, gate_b, sig_b, ALU.mult).then_inc(gs_rdy, 1)
                dve.wait_ge(gs_rdy, n + 1)
                if not first:
                    dve.wait_ge(at_mm, n)
                v.scalar_tensor_tensor(out=actv, in0=up_b, scalar=1.0, in1=gate_b, op0=ALU.add,
                                       op1=ALU.mult).then_inc(act_rdy, 1)

            def turned_lo(n, ev_sem, hi_part, lo_part, lo_sem):
                dve.wait_ge(ev_sem, n + 1)
                v.tensor_tensor(lo_part[:], ps[:, 4:6, :].rearrange("p b (k t) -> p (b k) t", k=4),
                                hi_part[:].bitcast(F32), ALU.subtract).then_inc(lo_sem, 1)

            def y_scaled(n, s, rnd, stored):
                dve.wait_ge(w_used[SLOTS - 1], rnd)
                if stored is not None:
                    dve.wait_ge(y_out[s], 16 * stored)
                v.tensor_tensor(two(ysb[s]), ps[:, 6:8, :], two(mod[5]), ALU.mult).then_inc(y_ev, 1)

            x_lo = lambda n: turned_lo(n, xt_ev, xTh, xTl, xt_lo)
            a_lo = lambda n: turned_lo(n, at_ev, aTh, aTl, at_lo)
            lo = lambda rnd: split_lo(dve, v, DVE_SLOTS, rnd)
            lo(1)
            x_lo(0)
            lo(2)
            lo(3)
            clamp(0, 2)
            x_lo(1)
            swiglu(0, first=True)
            a_lo(0)
            lo(4)
            lo(5)

            def step(n, s, stored):
                clamp(n - 1, up_round(n - 1) + 1)
                x_lo(n)
                swiglu(n - 1)
                lo(up_round(n))
                y_scaled(n - 2, s, down_round(n - 2), stored)
                a_lo(n - 1)
                lo(up_round(n) + 1)
                lo(down_round(n - 1))

            step(2, 0, None)
            step(3, 1, None)
            with dve.Fori(2, E // 2) as m:
                for s in range(2):
                    step(2 * m + s, s, m - 1)
            clamp(E - 1, up_round(E - 1) + 1)
            swiglu(E - 1)
            lo(LAST_DOWN)
            y_scaled(E - 2, 0, down_round(E - 2), E // 2 - 1)
            a_lo(E - 1)
            y_scaled(E - 1, 1, LAST_DOWN, E // 2 - 1)
            ov = overflow_count(dve)
            with dve.If(ov > 0):
                with dve.Fori(0, ov) as j:
                    x_lo(E + j)
                    lo(LAST_DOWN + 3 * j + 1)
                    lo(LAST_DOWN + 3 * j + 2)
                    clamp(E + j, LAST_DOWN + 3 * j + 2)
                    swiglu(E + j)
                    a_lo(E + j)
                    lo(LAST_DOWN + 3 * j + 3)
                    y_scaled(E + j, 0, LAST_DOWN + 3 * j + 3, E // 2 + j)
            dve.wait_ge(normf_in, 16)

            def total(t):
                y = yg[t % 3]
                c = comb[t % 2]
                dve.wait_ge(yg_in[t % 3], 16 * TOPK * (t // 3 + 1))
                if t >= 2:
                    dve.wait_ge(out_done[t % 2], 16)
                for k in range(TOPK):
                    ins = v.scalar_tensor_tensor(out=c, in0=y[k], scalar=gates[:, t, k:k + 1],
                                                 in1=c if k else x2[:, t, :], op0=ALU.mult, op1=ALU.add)
                    if k < TOPK - 1:
                        link(ins)
                ins.then_inc(x3_rdy, 1)

            def normed(t):
                c = comb[t % 2]
                dve.wait_ge(rms3_rdy, t + 1)
                link(v.reciprocal(rstd[:, t:t + 1], rstd[:, t:t + 1]))
                v.scalar_tensor_tensor(out=c, in0=c, scalar=rstd[:, t:t + 1], in1=normfB, op0=ALU.mult,
                                       op1=ALU.mult).then_inc(res_rdy, 1)

            for t in range(TT):
                total(t)
                if t:
                    normed(t - 1)
            normed(TT - 1)

        @block.tensor
        def _(pe):
            mm = nc.tensor.matmul

            def project(t):
                pe.wait_ge(wout_in, 16)
                if t == 0:
                    read_by(pe, ("pm", CT - 1))
                if t >= 2:
                    pe.wait_ge(x2_rdy, t - 1)
                for n, m in enumerate((2, 3, 4, 5, 6, 7, 0, 1)):
                    if t == 0 and m == 0:
                        pe.wait_ge(rw_out, 2)
                    for c in range(2):
                        ins = mm(ps[:, 2 * (t % 2) + c, :], mixed[m][:, P * t:P * t + P],
                                 w_out_sb[:, m, 512 * c:512 * c + 512], start=(n == 0), stop=(n == KT - 1))
                ins.then_inc(p_mm, 1)

            def turn(t):
                pe.wait_ge(h2_rdy, t + 1)
                if t:
                    pe.wait_ge(h2t_ev, t)
                for k in range(KT):
                    ins = nc.tensor.transpose(ps[:, 4 + k // 4, P * (k % 4):P * (k % 4) + P],
                                              h2[t % 2][:, P * k:P * k + P], ident[:])
                ins.then_inc(h2t_mm, 1)

            def router(t):
                pe.wait_ge(h2t_ev, t + 1)
                pe.wait_ge(small2_in, 16 * 5)
                for k in range(KT):
                    ins = mm(ps[:, 6 + t % 2, E * t:E * t + E], h2T[:, k, :], rw_sb[:, k, :], start=(k == 0), stop=(k == KT - 1))
                ins.then_inc(lg_mm, 1)

            project(0)
            project(1)
            for t in range(TT):
                turn(t)
                router(t)
                if t + 2 < TT:
                    project(t + 2)
            pe.wait_ge(mask_rdy, TT)
            for t in range(TT + 1):
                o = ps[:, 7, E * t:E * t + E]
                for j in range(min(t + 1, TT)):
                    lhs = strictb if j == t else onesb
                    ins = mm(o, lhs[:], maskb[:, j, :], start=(j == 0), stop=(j == min(t, TT - 1)))
            ins.then_inc(rank_mm, 1)
            for m in range(TT * TOPK):
                pe.wait_ge(onehots, m + 1)
                ins = mm(ps[:, 6, 0:NB], lane_oh[:, m, :], block_oh[:, m, :], start=(m == 0),
                         stop=(m == TT * TOPK - 1))
            ins.then_inc(tok_mm, 1)

            def xt(n, s, cnt):
                pe.wait_ge(xg_in[s], 16 * cnt)
                for k in range(KT):
                    ins = nc.tensor.transpose(ps[:, 4 + k // 4, P * (k % 4):P * (k % 4) + P],
                                              xg[s][:, P * k:P * k + P], ident[:])
                ins.then_inc(xt_mm, 1)

            def bias(banks, bank0, col, e):
                for c in range(banks):
                    mm(ps[:, bank0 + c, :], bsel[:, bass.ds(e, 1)].to_broadcast([3 * E, P]),
                       bparts[0:3 * E, col + 512 * c:col + 512 * c + 512], start=True, stop=False)

            def chunk(s, rnd, tiles, xh, xl, banks, bank0, last):
                pe.wait_ge(lo_rdy[s], rnd)
                for i, k in enumerate(tiles):
                    for x, parts in ((xh, (w_hi, w_lo)), (xl, (w_hi,))):
                        for c in range(banks):
                            for w in parts:
                                ins = mm(ps[:, bank0 + c, :], x[:, k, :],
                                         w[:, s, 512 * (banks * i + c):512 * (banks * i + c) + 512], start=False,
                                         stop=(last and i == len(tiles) - 1 and x is xl))
                ins.then_inc(w_used[s], 1)

            def gate_up(n, rnd, e):
                bias(4, 0, 0, e)
                pe.wait_ge(xt_lo, n + 1)
                for k in range(KT):
                    chunk(k % SLOTS, rnd if k < SLOTS else rnd + 1, (k,), xTh, xTl, 4, 0, k == KT - 1)

            def at(n):
                pe.wait_ge(act_rdy, n + 1)
                for k in range(KT):
                    ins = nc.tensor.transpose(ps[:, 4 + k // 4, P * (k % 4):P * (k % 4) + P],
                                              actv[:, P * k:P * k + P], ident[:])
                ins.then_inc(at_mm, 1)

            def down(n, rnd, e):
                bias(2, 6, 2 * F, e)
                pe.wait_ge(at_lo, n + 1)
                for s in range(SLOTS):
                    chunk(s, rnd, (2 * s, 2 * s + 1), aTh, aTl, 2, 6, s == SLOTS - 1)

            def step(n, s, cnt, yn):
                pe.wait_ge(at_lo, n - 1)
                xt(n, s, cnt)
                if yn is not None:
                    pe.wait_ge(y_ev, yn)
                down(n - 2, down_round(n - 2), n - 2)
                pe.wait_ge(xt_lo, n + 1)
                at(n - 1)
                pe.wait_ge(sw_rd, n)
                gate_up(n, up_round(n), n)

            pe.wait_ge(ov_rdy, 1)
            xt(0, 0, 1)
            gate_up(0, 1, 0)
            xt(1, 1, 1)
            pe.wait_ge(xt_lo, 2)
            at(0)
            pe.wait_ge(sw_rd, 1)
            gate_up(1, up_round(1), 1)
            step(2, 0, 2, None)
            step(3, 1, 2, 1)
            with pe.Fori(2, E // 2) as m:
                for s in range(2):
                    step(2 * m + s, s, m + 1, 2 * m + s - 2)
            pe.wait_ge(y_ev, E - 2)
            down(E - 2, down_round(E - 2), E - 2)
            at(E - 1)
            pe.wait_ge(y_ev, E - 1)
            down(E - 1, LAST_DOWN, E - 1)
            ov = overflow_count(pe)
            with pe.If(ov > 0):
                with pe.Fori(0, ov) as j:
                    n = E + j
                    rnd = LAST_DOWN + 3 * j + 1
                    e = pe.value_load(ovI[0:1, bass.ds(j, 1)], min_val=0, max_val=E - 1)
                    pe.wait_ge(at_lo, n)
                    xt(n, 0, E // 2 + 1 + j)
                    pe.wait_ge(sw_rd, n)
                    gate_up(n, rnd, e)
                    at(n)
                    pe.wait_ge(y_ev, n)
                    down(n, rnd + 2, e)


_INS = ["x", "c", "ada_w", "ada_b", "norm1", "w_in", "w_out", "rwkv_mu", "rwkv_w0", "rwkv_w_up", "rwkv_a0",
        "rwkv_a_up", "rwkv_g_up", "rwkv_k_k", "rwkv_k_a", "rwkv_r_k", "rwkv_ln_w", "rwkv_ln_b", "pool_w",
        "pool_scale", "fox_b_f", "norm2", "router_w", "router_b", "moe_w_gu", "moe_b_gu", "moe_w_down",
        "moe_b_down", "norm_f"]


def kernel(**inputs):
    import concourse.bacc as _bacc
    from concourse.bass_utils import run_bass_kernel_spmd as _run

    nc = _bacc.Bacc("TRN2", target_bir_lowering=False, num_devices=1)
    arrays, args = {}, {}
    for name in _INS:
        arr = np.ascontiguousarray(inputs[name])
        arrays[f"in_{name}"] = arr
        args[name] = nc.dram_tensor(f"in_{name}", arr.shape, mybir.dt.from_np(arr.dtype), kind="ExternalInput").ap()
    out = nc.dram_tensor("out", (1, S, D), F32, kind="ExternalOutput").ap()
    build(nc, args, out)
    r = _run(nc, [arrays], core_ids=[0])
    return r.results[0]["out"]
```
